# Optimizing a Trainium2 kernel written in Bass

```python
import math
import jax, jax.numpy as jnp
from jax import lax
import numpy as np

D_MODEL = 2048
BATCH = 1
SEQ = 256
DEPTH = 1

MEM_LEN = 256
HEAD_DIM = 128
DIFF_HEADS = 8
DIFF_HALF = HEAD_DIM // 2
DIFF_WIDTH = DIFF_HEADS * HEAD_DIM
MOBA_HEADS = 8
MOBA_WIDTH = MOBA_HEADS * HEAD_DIM
D_MIX = DIFF_WIDTH + MOBA_WIDTH
IN_COLS = 3 * DIFF_WIDTH + 3 * MOBA_WIDTH + D_MIX
MOBA_BLOCK = 256
MOBA_TOPK = 3
MOBA_Q_CHUNK = 32
DENSE_Q_BLOCK = 128
MEM_HEADS = 4
MEM_WIDTH = MEM_HEADS * HEAD_DIM
EPS = 1e-6
SPLITS = [DIFF_WIDTH, 2 * DIFF_WIDTH, 3 * DIFF_WIDTH,
          3 * DIFF_WIDTH + MOBA_WIDTH, 3 * DIFF_WIDTH + 2 * MOBA_WIDTH,
          3 * DIFF_WIDTH + 3 * MOBA_WIDTH]

kernel_name = "hybrid_diffattn_moba_gated_memxattn"

def rmsnorm(x, g):
    xf = x.astype(jnp.float32)
    r = lax.rsqrt(jnp.mean(xf * xf, axis=-1, keepdims=True) + EPS)
    return (xf * r).astype(x.dtype) * g

def alibi_slopes(n):
    return jnp.asarray(2.0 ** (-8.0 * np.arange(1, n + 1) / n), dtype=jnp.float32)

def diff_attention(q, k, v, lam, subln_g, lam_init, slopes):
    B, H, S = q.shape[:3]
    nqb = S // DENSE_Q_BLOCK
    scale = DIFF_HALF ** -0.5
    kpos = jnp.arange(S)
    qb = q.reshape(B, H, nqb, DENSE_Q_BLOCK, 2, DIFF_HALF).transpose(2, 0, 1, 3, 4, 5)

    def one_block(args):
        i, qi = args
        qpos = i * DENSE_Q_BLOCK + jnp.arange(DENSE_Q_BLOCK)
        dist = (qpos[:, None] - kpos[None, :]).astype(jnp.float32)
        bias = -slopes[:, None, None] * dist
        logits = jnp.einsum('bhqcd,bhkcd->bhcqk', qi, k).astype(jnp.float32) * scale
        logits = jnp.where(dist >= 0, logits + bias[None, :, None], -jnp.inf)
        p = jax.nn.softmax(logits, axis=-1)
        attn = p[:, :, 0] - lam.astype(jnp.float32) * p[:, :, 1]
        return jnp.einsum('bhqk,bhkd->bhqd', attn.astype(v.dtype), v)

    o = lax.map(one_block, (jnp.arange(nqb), qb))
    o = o.transpose(1, 2, 0, 3, 4).reshape(B, H, S, HEAD_DIM)
    return rmsnorm(o, subln_g) * (1.0 - lam_init)

def moba_attention(q, k, v, slopes):
    B, H, S, D = q.shape
    nb = -(-S // MOBA_BLOCK)
    pad = nb * MOBA_BLOCK - S
    scale = D ** -0.5
    tk = min(MOBA_TOPK, nb)
    kpad = jnp.pad(k, ((0, 0), (0, 0), (0, pad), (0, 0)))
    vpad = jnp.pad(v, ((0, 0), (0, 0), (0, pad), (0, 0)))
    kb = kpad.reshape(B, H, nb, MOBA_BLOCK, D)
    vb = vpad.reshape(B, H, nb, MOBA_BLOCK, D)
    kmean = jnp.mean(kb.astype(jnp.float32), axis=3)
    nqc = S // MOBA_Q_CHUNK
    qc = q.reshape(B, H, nqc, MOBA_Q_CHUNK, D).transpose(2, 0, 1, 3, 4)
    bi = jnp.arange(B)[:, None, None, None]
    hi = jnp.arange(H)[None, :, None, None]
    blk = jnp.arange(MOBA_BLOCK)

    def one_chunk(args):
        i, qi = args
        start = i * MOBA_Q_CHUNK
        cur = start // MOBA_BLOCK
        qpos = start + jnp.arange(MOBA_Q_CHUNK)
        gate = jnp.einsum('bhqd,bhnd->bhqn', qi.astype(jnp.float32), kmean)
        gate = jnp.where(jnp.arange(nb) < cur, gate, -jnp.inf)
        _, idx = lax.top_k(gate, tk)
        valid = idx < cur
        kg = kb[bi, hi, idx]
        vg = vb[bi, hi, idx]
        lg = jnp.einsum('bhqd,bhqjsd->bhqjs', qi, kg).astype(jnp.float32) * scale
        spos = idx[..., None] * MOBA_BLOCK + blk
        gdist = (qpos[None, None, :, None, None] - spos).astype(jnp.float32)
        lg = lg - slopes[None, :, None, None, None] * gdist
        lg = jnp.where(valid[..., None], lg, -jnp.inf).reshape(B, H, MOBA_Q_CHUNK, tk * MOBA_BLOCK)
        own_k = lax.dynamic_slice_in_dim(kpad, cur * MOBA_BLOCK, MOBA_BLOCK, axis=2)
        own_v = lax.dynamic_slice_in_dim(vpad, cur * MOBA_BLOCK, MOBA_BLOCK, axis=2)
        lo = jnp.einsum('bhqd,bhsd->bhqs', qi, own_k).astype(jnp.float32) * scale
        odist = (qpos[:, None] - (cur * MOBA_BLOCK + blk)[None, :]).astype(jnp.float32)
        lo = jnp.where(odist >= 0, lo - slopes[:, None, None] * odist, -jnp.inf)
        p = jax.nn.softmax(jnp.concatenate([lg, lo], axis=-1), axis=-1)
        pg = p[..., :tk * MOBA_BLOCK].reshape(B, H, MOBA_Q_CHUNK, tk, MOBA_BLOCK).astype(v.dtype)
        po = p[..., tk * MOBA_BLOCK:].astype(v.dtype)
        return (jnp.einsum('bhqjs,bhqjsd->bhqd', pg, vg)
                + jnp.einsum('bhqs,bhsd->bhqd', po, own_v))

    o = lax.map(one_chunk, (jnp.arange(nqc), qc))
    return o.transpose(1, 2, 0, 3, 4).reshape(B, H, S, D)

def setup_inputs(seed: int = 0) -> dict:
    key = jax.random.key(seed)
    ks = jax.random.split(key, 16)
    f32 = jnp.float32

    def w(k, shape, fan_in):
        return jax.random.normal(k, shape, f32) * fan_in ** -0.5

    def gain(k, shape):
        return 1.0 + 0.02 * jax.random.normal(k, shape, f32)

    return {
        "x": jax.random.normal(ks[0], (BATCH, SEQ, D_MODEL), f32),
        "mem": jax.random.normal(ks[1], (BATCH, MEM_LEN, D_MODEL), f32),
        "norm_mix_g": gain(ks[2], (DEPTH, D_MODEL)),
        "w_in": w(ks[3], (DEPTH, D_MODEL, IN_COLS), D_MODEL),
        "lambda_q1": 0.1 * jax.random.normal(ks[4], (DEPTH, DIFF_HALF), f32),
        "lambda_k1": 0.1 * jax.random.normal(ks[5], (DEPTH, DIFF_HALF), f32),
        "lambda_q2": 0.1 * jax.random.normal(ks[6], (DEPTH, DIFF_HALF), f32),
        "lambda_k2": 0.1 * jax.random.normal(ks[7], (DEPTH, DIFF_HALF), f32),
        "subln_g": gain(ks[8], (DEPTH, HEAD_DIM)),
        "w_out": w(ks[9], (DEPTH, D_MIX, D_MODEL), D_MIX),
        "norm_mem_g": gain(ks[10], (DEPTH, D_MODEL)),
        "mem_norm_g": gain(ks[11], (DEPTH, D_MODEL)),
        "w_q_mem": w(ks[12], (DEPTH, D_MODEL, MEM_WIDTH), D_MODEL),
        "w_kv_mem": w(ks[13], (DEPTH, D_MODEL, 2 * MEM_WIDTH), D_MODEL),
        "w_o_mem": w(ks[14], (DEPTH, MEM_WIDTH, D_MODEL), MEM_WIDTH),
        "final_g": gain(ks[15], (D_MODEL,)),
    }

def reference(x, mem, norm_mix_g, w_in, lambda_q1, lambda_k1, lambda_q2, lambda_k2,
              subln_g, w_out, norm_mem_g, mem_norm_g, w_q_mem, w_kv_mem, w_o_mem, final_g):
    B, S, _ = x.shape
    M = mem.shape[1]
    diff_slopes = alibi_slopes(DIFF_HEADS)
    moba_slopes = alibi_slopes(MOBA_HEADS)
    for l in range(DEPTH):
        h = rmsnorm(x, norm_mix_g[l])
        proj = jnp.einsum('bsd,de->bse', h, w_in[l])
        dq, dk, dv, mq, mk, mv, gate = jnp.split(proj, SPLITS, axis=-1)
        dq = dq.reshape(B, S, DIFF_HEADS, 2, DIFF_HALF).transpose(0, 2, 1, 3, 4)
        dk = dk.reshape(B, S, DIFF_HEADS, 2, DIFF_HALF).transpose(0, 2, 1, 3, 4)
        dv = dv.reshape(B, S, DIFF_HEADS, HEAD_DIM).transpose(0, 2, 1, 3)
        lam_init = 0.8 - 0.6 * math.exp(-0.3 * l)
        lam = (jnp.exp(jnp.sum(lambda_q1[l].astype(jnp.float32) * lambda_k1[l].astype(jnp.float32)))
               - jnp.exp(jnp.sum(lambda_q2[l].astype(jnp.float32) * lambda_k2[l].astype(jnp.float32)))
               + lam_init)
        d_out = diff_attention(dq, dk, dv, lam, subln_g[l], lam_init, diff_slopes)
        d_out = d_out.transpose(0, 2, 1, 3).reshape(B, S, DIFF_WIDTH)
        mq = mq.reshape(B, S, MOBA_HEADS, HEAD_DIM).transpose(0, 2, 1, 3)
        mk = mk.reshape(B, S, MOBA_HEADS, HEAD_DIM).transpose(0, 2, 1, 3)
        mv = mv.reshape(B, S, MOBA_HEADS, HEAD_DIM).transpose(0, 2, 1, 3)
        m_out = moba_attention(mq, mk, mv, moba_slopes)
        m_out = m_out.transpose(0, 2, 1, 3).reshape(B, S, MOBA_WIDTH)
        y = jnp.concatenate([d_out, m_out], axis=-1) * jax.nn.silu(gate)
        x = x + jnp.einsum('bse,ed->bsd', y, w_out[l])
        h2 = rmsnorm(x, norm_mem_g[l])
        mn = rmsnorm(mem, mem_norm_g[l])
        q = jnp.einsum('bsd,de->bse', h2, w_q_mem[l]).reshape(B, S, MEM_HEADS, HEAD_DIM)
        kv = jnp.einsum('bmd,de->bme', mn, w_kv_mem[l])
        km, vm = jnp.split(kv, 2, axis=-1)
        km = km.reshape(B, M, MEM_HEADS, HEAD_DIM)
        vm = vm.reshape(B, M, MEM_HEADS, HEAD_DIM)
        logits = jnp.einsum('bshd,bmhd->bhsm', q, km).astype(jnp.float32) * HEAD_DIM ** -0.5
        p = jax.nn.softmax(logits, axis=-1).astype(vm.dtype)
        o = jnp.einsum('bhsm,bmhd->bshd', p, vm).reshape(B, S, MEM_WIDTH)
        x = x + jnp.einsum('bse,ed->bsd', o, w_o_mem[l])
    return rmsnorm(x, final_g)


_drawn_inputs = setup_inputs


def setup_inputs(seed=0):
    import zlib

    import numpy as np

    out = dict(_drawn_inputs(seed))
    spreads = {}
    factors = {'norm_mix_g': 4.109,
     'lambda_k1': 5.593,
     'lambda_q2': 5.852,
     'subln_g': 8.0,
     'norm_mem_g': 8.0,
     'mem_norm_g': 8.0,
     'final_g': 2.744}
    for name, (base, spread) in spreads.items():
        noise = np.random.default_rng([zlib.crc32(name.encode()), seed]).standard_normal(out[name].shape)
        drawn = base * np.exp(spread * noise) if base else spread * noise
        out[name] = __import__('jax').numpy.asarray(drawn.astype(out[name].dtype))
    for name, factor in factors.items():
        out[name] = (out[name] * factor).astype(out[name].dtype)
    return out
```

```python
from contextlib import ExitStack

import concourse.bass as bass
from concourse import mybir

F32 = mybir.dt.float32
F32R = mybir.dt.float32r
I32 = mybir.dt.int32
ACT = mybir.ActivationFunctionType
ALU = mybir.AluOpType
AX = mybir.AxisListType

P = 128
SEQ = 256
DM = 2048
NT = SEQ // P
KO = DM // P
COLS = 512
GK = 4
NG = KO // GK
HEADS = 8
PAIRS = 2 * HEADS // 2
KIND_PAIRS = HEADS // 2
HALF_D = P // 2
PAIR_HALVES = 4 * NG
SPLITS = 4
RAW = 4
EPS = 1e-6
LAM_INIT = 0.2
MASKED = -3.0e38
DIFF_SCALE = float(HALF_D) ** -0.5
HEAD_SCALE = float(P) ** -0.5
RSQRT_SEED = float(0x5F3759DF)
RSQRT_STEPS = 10


class Kind:

    def __init__(self, name, maps, scale, first_pair):
        self.name, self.maps, self.scale, self.first_pair = name, maps, scale, first_pair
        self.diff = maps == 2


DIFF = Kind("diff", 2, DIFF_SCALE, 0)
MOBA = Kind("moba", 1, HEAD_SCALE, KIND_PAIRS)

TAIL = ([("out", 0, g) for g in range(3)] + [("out", 1, g) for g in range(3)]
        + [("out", 0, 3), ("out", 1, 3), ("out", 2, 0), ("out", 2, 1), ("out", 2, 2), ("qm", 0, 0),
           ("out", 2, 3), ("qm", 0, 1), ("out", 3, 0), ("out", 3, 1), ("qm", 0, 2), ("out", 3, 2),
           ("out", 3, 3), ("km", 0, 0), ("km", 0, 1), ("qm", 0, 3), ("km", 0, 2), ("km", 0, 3)]
        + [("vm", 0, g) for g in range(4)] + [("wo", n, 0) for n in range(4)])
TAIL_GROUP0 = PAIRS * 2 * NG
TAIL_HALF0 = 2 * TAIL_GROUP0
ALL_GROUPS = TAIL_GROUP0 + len(TAIL)

BLOCKS = ([("x", 0, 4), ("x", 1, 6), ("x", 2, 4), ("x", 3, 6)]
          + [("mem", 0, 4), ("mem", 1, 6), ("x1", 0, 4), ("mem", 2, 6), ("mem", 3, 4),
             ("x1", 1, 4), ("x1", 2, 4), ("x1", 3, 4)])
BLOCK_AFTER = {6: 4, 7: 5, 8: 6, 9: 7, 10: 8, 11: 9, 14: 10, 19: 11}


def done_at(what, n, g):
    return TAIL_HALF0 + 2 * (TAIL.index((what, n, g)) + 1)


def wait(engine, semaphore, value):
    if isinstance(value, int) and value <= 0:
        return
    engine.wait_ge(semaphore, value)


def program(nc, x, mem, norm_mix_g, w_in, lambda_q1, lambda_k1, lambda_q2, lambda_k2,
            subln_g, w_out, norm_mem_g, mem_norm_g, w_q_mem, w_kv_mem, w_o_mem, final_g, out):
    with ExitStack() as ctx:
        def sbuf(name, shape, dtype=F32):
            return ctx.enter_context(nc.sbuf_tensor(name, shape, dtype))

        def sem(name):
            return ctx.enter_context(nc.semaphore(name))

        w_raw = sbuf("w_raw", [P, RAW, GK, COLS])
        w_hi = sbuf("w_hi", [P, SPLITS, GK // 2, COLS], F32R)
        w_lo = sbuf("w_lo", [P, SPLITS, GK // 2, COLS], F32R)
        aT_hi = sbuf("aT_hi", [P, KO, SEQ], F32R)
        aT_lo = sbuf("aT_lo", [P, KO, SEQ], F32R)
        yT_hi = sbuf("yT_hi", [P, KO, SEQ], F32R)
        yT_lo = sbuf("yT_lo", [P, KO, SEQ], F32R)
        cT_hi = sbuf("cT_hi", [P, GK, SEQ], F32R)
        cT_lo = sbuf("cT_lo", [P, GK, SEQ], F32R)
        xs = sbuf("xs", [P, NT, DM])
        mems = sbuf("mems", [P, NT, DM])
        final_gs = sbuf("final_gs", [P, DM])
        pool = sbuf("pool", [P, 6912])
        ident = sbuf("ident", [P, P])
        dist = sbuf("dist", [P, SEQ])
        slopes = sbuf("slopes", [P, 2 * HEADS])
        gains = sbuf("gains", [3 * KO + 1, P])
        gainsT = sbuf("gainsT", [P, 3 * KO + 1])
        small = sbuf("small", [P, 160])

        def carve(tensor, start, *shape):
            size = 1
            for s in shape:
                size *= s
            flat = tensor[:, start:start + size]
            if len(shape) == 1:
                return flat, start + size
            names = "abcd"[:len(shape)]
            view = flat.rearrange(f"p ({' '.join(names)}) -> p {' '.join(names)}",
                                  **{n: s for n, s in zip(names, shape)})
            return view, start + size

        qk_sb, at = carve(pool, 0, NT, COLS)
        v_sb, at = carve(pool, at, NT, 2 * P)
        gate_sb, at = carve(pool, at, NT, 2 * P)
        sig_sb, at = carve(pool, at, NT, 2 * P)
        qT_sb, at = carve(pool, at, 2, SEQ)
        kT_sb, at = carve(pool, at, 2, SEQ)
        prob_sb, at = carve(pool, at, 2, 2, SEQ + P)
        probT_sb, at = carve(pool, at, 2, 3, P)
        y_sb, at = carve(pool, at, NT, 2 * P)
        junk, at = carve(pool, at, COLS)
        assert at <= 6912
        junk_row, _ = carve(pool, 0, DM)
        lam_in, _ = carve(pool, DM, 4, HALF_D)
        lam_prod, _ = carve(pool, DM + 4 * HALF_D, 2, HALF_D)
        qm_sb, at = carve(pool, 0, NT, COLS)
        km_sb, at = carve(pool, at, NT, COLS)
        vm_sb, at = carve(pool, at, NT, COLS)
        qmT_sb, at = carve(pool, at, 4, SEQ)
        kmT_sb, at = carve(pool, at, 4, SEQ)
        o_sb, at = carve(pool, at, NT, COLS)
        assert at <= 6912 - COLS
        mem_flat = mems[:, :, :].rearrange("p t d -> p (t d)")
        pm_sb, at = carve(mem_flat, 0, NT, 4, SEQ)
        pmT_sb, at = carve(mem_flat, at, NT, 2, 4, P)

        def columns(start, *shape):
            return carve(small, start, *shape)

        x_sq, at = columns(0, NT)
        x_ms, at = columns(at, NT)
        r_x, at = columns(at, NT)
        neg_r_x, at = columns(at, NT)
        newton, at = columns(at, 4)
        neg_max, at = columns(at, 2, 2, 2)
        exp_sum, at = columns(at, 2, 2, 2)
        inv_sum1, at = columns(at, 2, 2)
        mix, at = columns(at, 2, 2)
        inv_sum0, at = columns(at, 2, 2)
        inv_sq, at = columns(at, 2, 2)
        o_sq, at = columns(at, 2, 2)
        o_ms, at = columns(at, 2, 2)
        r_o, at = columns(at, 2, 2)
        y_scale, at = columns(at, 2, 2)
        lam_dot, at = columns(at, 2)
        lam_exp, at = columns(at, 2)
        neg_lam, at = columns(at, 1)
        mem_sq4, at = columns(at, NT, 4)
        mem_sq, at = columns(at, NT)
        sub_gain, at = columns(at, 1)
        x1_tot, at = columns(at, NT)
        x2_tot, at = columns(at, NT)
        mem_ms, at = columns(at, NT)
        r_mem, at = columns(at, NT)
        x1_sq, at = columns(at, NT, 4)
        x1_ms, at = columns(at, NT)
        r_x1, at = columns(at, NT)
        q_scale, at = columns(at, NT)
        neg_max_m, at = columns(at, NT, 4)
        sum_m, at = columns(at, NT, 4)
        inv_sum_m, at = columns(at, NT, 4)
        x2_sq, at = columns(at, NT, 4)
        x2_ms, at = columns(at, NT)
        r_x2, at = columns(at, NT)
        assert at <= 160

        ps = ctx.enter_context(nc.psum_tensor("ps", [P, 8, COLS], F32))

        x_loaded = [sem(f"x_loaded{n}") for n in range(4)]
        mem_loaded = sem("mem_loaded")
        gains_loaded = sem("gains_loaded")
        lam_loaded = sem("lam_loaded")
        final_g_loaded = sem("final_g_loaded")
        group_loaded = [sem(f"group_loaded{s}") for s in range(RAW)]
        hi_made = sem("hi_made")
        lo_made = sem("lo_made")
        half_done = sem("half_done")
        ident_ready = sem("ident_ready")
        consts_ready = sem("consts_ready")
        gainsT_made = sem("gainsT_made")
        gainsT_ready = sem("gainsT_ready")
        block_made = sem("block_made")
        block_hi = sem("block_hi")
        block_lo = sem("block_lo")
        x_summed = sem("x_summed")
        x_ms_ready = sem("x_ms_ready")
        r_x_steps = sem("r_x_steps")
        r_x_ready = sem("r_x_ready")
        lam_steps = sem("lam_steps")
        lam_dots = sem("lam_dots")
        lam_exps = sem("lam_exps")
        lam_ready = sem("lam_ready")
        qk0_ready = sem("qk0_ready")
        qk1_ready = sem("qk1_ready")
        gate_ready = sem("gate_ready")
        v_ready = sem("v_ready")
        silu_steps = sem("silu_steps")
        qkT_made = sem("qkT_made")
        qT_ready = sem("qT_ready")
        kT_ready = sem("kT_ready")
        scores_made = sem("scores_made")
        logits_ready = sem("logits_ready")
        max_ready = sem("max_ready")
        exp_ready = sem("exp_ready")
        mix_steps = sem("mix_steps")
        attn_ready = sem("attn_ready")
        probT_made = sem("probT_made")
        probT_ready = sem("probT_ready")
        pv_made = sem("pv_made")
        o_summed = sem("o_summed")
        y_steps = {"diff": sem("y_steps_diff"), "moba": sem("y_steps_moba")}
        y_ready = sem("y_ready")
        yT_made = sem("yT_made")
        yT_hi_ready = sem("yT_hi_ready")
        yT_ready = sem("yT_ready")
        mem_summed = sem("mem_summed")
        r_mem_steps = sem("r_mem_steps")
        x1_ready = sem("x1_ready")
        x1_summed = sem("x1_summed")
        r_x1_steps = sem("r_x1_steps")
        q_scale_ready = sem("q_scale_ready")
        qm_ready = sem("qm_ready")
        qmT_made = sem("qmT_made")
        qmT_ready = sem("qmT_ready")
        km_ready = sem("km_ready")
        kmT_made = sem("kmT_made")
        kmT_ready = sem("kmT_ready")
        vm_ready = sem("vm_ready")
        scores_m_made = sem("scores_m_made")
        max_m_ready = sem("max_m_ready")
        exp_m_ready = sem("exp_m_ready")
        inv_m_ready = sem("inv_m_ready")
        pmT_made = sem("pmT_made")
        pmT_ready = [sem("pmT_ready_act"), sem("pmT_ready_dve")]
        om_made = sem("om_made")
        om_ready = sem("om_ready")
        omT_made = sem("omT_made")
        omT_hi_ready = sem("omT_hi_ready")
        omT_ready = sem("omT_ready")
        x2_ready = sem("x2_ready")
        x2_summed = sem("x2_summed")
        x2_gained = sem("x2_gained")
        r_x2_steps = sem("r_x2_steps")
        out_ready = [sem(f"out_ready{t}") for t in range(NT)]
        out_stored = sem("out_stored")

        rows = "(g k p) n -> g p k n"
        in_slabs = w_in[0].rearrange("(g k p) (s c) -> g p k s c", k=GK, p=P, c=HEADS * P)
        tail_groups = {"out": w_out[0].rearrange(rows, k=GK, p=P),
                       "qm": w_q_mem[0].rearrange(rows, k=GK, p=P),
                       "km": w_kv_mem[0].rearrange(rows, k=GK, p=P),
                       "vm": w_kv_mem[0].rearrange(rows, k=GK, p=P),
                       "wo": w_o_mem[0].rearrange(rows, k=GK, p=P)}
        x_tiles = x[0].rearrange("(t p) d -> p t d", p=P)
        mem_tiles = mem[0].rearrange("(t p) d -> p t d", p=P)
        out_tiles = out[0].rearrange("(t p) d -> p t d", p=P)

        block = ctx.enter_context(nc.Block())

        @block.sync
        def _(sp):
            def load_pair_group(kind, pair, local, g):
                first = {("diff", 0): 0, ("diff", 1): 2, ("moba", 0): 3, ("moba", 1): 5}[kind.name, g // NG]
                second = {("diff", 0): 1, ("diff", 1): 6, ("moba", 0): 4, ("moba", 1): 7}[kind.name, g // NG]
                wait(sp, lo_made, PAIR_HALVES * pair + 2 * (g - RAW + 1))
                for part, slab in enumerate((first, second)):
                    sp.dma_start(w_raw[:, g % RAW, :, part * 2 * P:(part + 1) * 2 * P],
                                 in_slabs[g % NG][:, :, slab, bass.ds(2 * P * local, 2 * P)]
                                 ).then_inc(group_loaded[g % RAW], 16)

            def load_x(n):
                sp.dma_start(xs[:, :, n * COLS:(n + 1) * COLS],
                             x_tiles[:, :, n * COLS:(n + 1) * COLS]).then_inc(x_loaded[n], 16)

            load_x(0)
            load_x(1)
            load_pair_group(DIFF, 0, 0, 0)
            load_x(2)
            load_x(3)
            for g in range(1, 2 * NG):
                load_pair_group(DIFF, 0, 0, g)
            with sp.Fori(1, KIND_PAIRS) as j:
                for g in range(2 * NG):
                    load_pair_group(DIFF, j, j, g)
            with sp.Fori(KIND_PAIRS, PAIRS) as j:
                for g in range(2 * NG):
                    load_pair_group(MOBA, j, j - KIND_PAIRS, g)
            sp.dma_start(mems[:, :, :], mem_tiles).then_inc(mem_loaded, 16)
            for w, (what, n, g) in enumerate(TAIL):
                group = TAIL_GROUP0 + w
                first_col = n * COLS + (COLS if what == "vm" else 0)
                sp.wait_ge(lo_made, 2 * (group - RAW + 1))
                for part in range(2):
                    cols = slice(first_col + part * 2 * P, first_col + (part + 1) * 2 * P)
                    sp.dma_start(w_raw[:, group % RAW, :, part * 2 * P:(part + 1) * 2 * P],
                                 tail_groups[what][g][:, :, cols]).then_inc(group_loaded[group % RAW], 16)
            for t in range(NT):
                sp.wait_ge(out_ready[t], 1)
                sp.dma_start(out_tiles[:, t, :], xs[:, t, :]).then_inc(out_stored, 16)
            sp.wait_ge(out_stored, 16 * NT)

        @block.gpsimd
        def _(pool_e):
            pool_e.memset(ident[:, :], 0.0).then_inc(ident_ready, 1)
            pool_e.iota(dist[:, :], pattern=[[1, SEQ]], base=-P, channel_multiplier=-1,
                        allow_small_or_imprecise_dtypes=True).then_inc(consts_ready, 1)
            pool_e.wait_ge(ident_ready, 1)
            pool_e.affine_select(out=ident[:, :], in_=ident[:, :], compare_op=ALU.not_equal, fill=1.0,
                                 base=0, pattern=[[-1, P]], channel_multiplier=1).then_inc(ident_ready, 1)
            pool_e.wait_ge(consts_ready, 1)
            pool_e.affine_select(out=dist[:, :], in_=dist[:, :], compare_op=ALU.is_ge, fill=MASKED,
                                 base=P, pattern=[[-1, SEQ]], channel_multiplier=1).then_inc(consts_ready, 1)
            for h in range(HEADS):
                for kind in range(2):
                    pool_e.memset(slopes[:, kind * HEADS + h:kind * HEADS + h + 1],
                                  2.0 ** (-8.0 * (h + 1) / HEADS)).then_inc(consts_ready, 1)

        CONSTS = 2 + 2 * HEADS

        @block.tensor
        def _(pe):
            def half_group(half, slot, banks, hi, lo, k0, first, last):
                wait(pe, lo_made, half + 1)
                for k in range(GK // 2):
                    for t in range(NT):
                        tok = slice(t * P, (t + 1) * P)
                        acc = ps[:, banks[t], :]
                        pe.matmul(acc, hi[:, k0 + k, tok], w_hi[:, slot, k], start=first and k == 0, stop=False)
                        pe.matmul(acc, hi[:, k0 + k, tok], w_lo[:, slot, k], start=False, stop=False)
                        m = pe.matmul(acc, lo[:, k0 + k, tok], w_hi[:, slot, k], start=False,
                                      stop=last and k == GK // 2 - 1)
                m.then_inc(half_done, 1)

            def transpose_block(b):
                source, n, bank = BLOCKS[b]
                rows_of = {"x": xs, "mem": mems, "x1": xs}[source]
                before = [c for c in range(b) if BLOCKS[c][2] == bank]
                if source == "x":
                    pe.wait_ge(x_loaded[n], 16)
                if source == "mem":
                    pe.wait_ge(mem_loaded, 16)
                if source == "x1":
                    pe.wait_ge(x1_ready, NT * (n + 1))
                if before:
                    pe.wait_ge(block_lo, 2 * (before[-1] + 1))
                for i in range(2):
                    for k in range(2):
                        for t in range(NT):
                            col = n * COLS + (2 * i + k) * P
                            m = pe.transpose(ps[:, bank + i, (k * NT + t) * P:(k * NT + t + 1) * P],
                                             rows_of[:, t, col:col + P], ident[:, :])
                    m.then_inc(block_made, 1)

            def attend(n, a, kind, yT_after):
                x_bank, y_bank = (6, 4), (7, 5)
                if n == 0:
                    for part in range(2):
                        for u in range(2):
                            for t in range(NT):
                                col = (part * 2 + u) * P
                                m = pe.transpose(ps[:, 4 + part, (u * NT + t) * P:(u * NT + t + 1) * P],
                                                 qk_sb[:, t, col:col + P], ident[:, :])
                        m.then_inc(qkT_made, 1)
                if n in (2, 3):
                    u = n - 2
                    if u == 0:
                        pe.wait_ge(qT_ready, a + 1)
                        pe.wait_ge(kT_ready, a + 1)
                        wait(pe, yT_ready, a)
                    banks = (x_bank[u], y_bank[u])
                    for t in (1, 0):
                        for c in range(kind.maps):
                            part = slice(c * HALF_D, (c + 1) * HALF_D) if kind.diff else slice(0, P)
                            keys = (t + 1) * P
                            col = 0 if t == 1 else SEQ
                            m = pe.matmul(ps[:, banks[c], col:col + keys], qT_sb[part, u, t * P:(t + 1) * P],
                                          kT_sb[part, u, 0:keys], start=True, stop=True)
                    m.then_inc(scores_made, 1)
                if n in (6, 8):
                    u = (n - 6) // 2
                    pe.wait_ge(attn_ready if kind.diff else exp_ready, 2 * a + u + 1)
                    for i, col in enumerate((SEQ, 0, P)):
                        m = pe.transpose(ps[:, x_bank[u], i * P:(i + 1) * P], prob_sb[:, u, 0, col:col + P],
                                         ident[:, :])
                    m.then_inc(probT_made, 1)
                if n in (7, 9):
                    u = (n - 7) // 2
                    pe.wait_ge(probT_ready, 2 * a + u + 1)
                    if u == 0:
                        pe.wait_ge(v_ready, a + 1)
                    head = slice(u * P, (u + 1) * P)
                    pe.matmul(ps[:, y_bank[u], 0:P], probT_sb[:, u, 0], v_sb[:, 0, head], start=True, stop=True)
                    pe.matmul(ps[:, y_bank[u], P:2 * P], probT_sb[:, u, 1], v_sb[:, 0, head], start=True, stop=False)
                    pe.matmul(ps[:, y_bank[u], P:2 * P], probT_sb[:, u, 2], v_sb[:, 1, head],
                              start=False, stop=True).then_inc(pv_made, 1)
                if n == yT_after:
                    pe.wait_ge(y_ready, a + 1)
                    for u in range(2):
                        for t in range(NT):
                            m = pe.transpose(ps[:, 6, (u * NT + t) * P:(u * NT + t + 1) * P],
                                             y_sb[:, t, u * P:(u + 1) * P], ident[:, :])
                    m.then_inc(yT_made, 1)

            def project_pair(j, kind):
                for n in range(PAIR_HALVES):
                    if n == 0:
                        wait(pe, qk0_ready, j)
                        wait(pe, qk1_ready, j)
                    if n == PAIR_HALVES // 2:
                        wait(pe, v_ready, j)
                    within = n % (2 * NG)
                    if kind is None and n < 2 * NG:
                        pe.wait_ge(block_lo, n + 1)
                    half_group(PAIR_HALVES * j + n, n % SPLITS, (0, 1) if n < 2 * NG else (2, 3),
                               aT_hi, aT_lo, within * (GK // 2), within == 0, within == 2 * NG - 1)
                    if kind is None:
                        if n in (0, 1):
                            transpose_block(2 + n)
                    else:
                        attend(n, j - 1, kind, 13)

            pe.wait_ge(ident_ready, 2)
            pe.wait_ge(gains_loaded, 64)
            pe.transpose(ps[:, 3, 0:3 * KO + 1], gains[:, :], ident[0:3 * KO + 1, 0:3 * KO + 1]
                         ).then_inc(gainsT_made, 1)
            transpose_block(0)
            transpose_block(1)
            project_pair(0, None)
            with pe.Fori(1, KIND_PAIRS + 1) as j:
                project_pair(j, DIFF)
            with pe.Fori(KIND_PAIRS + 1, PAIRS) as j:
                project_pair(j, MOBA)

            banks_of = {("out", 0): (0, 1), ("out", 1): (2, 3), ("out", 2): (0, 1), ("out", 3): (2, 3),
                        ("qm", 0): (6, 7), ("km", 0): (0, 1), ("vm", 0): (2, 3),
                        ("wo", 0): (2, 3), ("wo", 1): (0, 1), ("wo", 2): (4, 5), ("wo", 3): (6, 7)}
            operand = {"out": (yT_hi, yT_lo), "qm": (cT_hi, cT_lo), "km": (aT_hi, aT_lo),
                       "vm": (aT_hi, aT_lo), "wo": (cT_hi, cT_lo)}
            for w, (what, n, g) in enumerate(TAIL):
                if (what, n, g) == ("out", 0, 0):
                    pe.wait_ge(qk0_ready, PAIRS)
                    pe.wait_ge(qk1_ready, PAIRS)
                if (what, n, g) == ("out", 1, 0):
                    pe.wait_ge(v_ready, PAIRS)
                if (what, n, g) == ("out", 0, 3):
                    pe.wait_ge(yT_ready, PAIRS)
                if (what, n, g) == ("out", 2, 0):
                    pe.wait_ge(x1_ready, NT * 1)
                if (what, n, g) == ("out", 3, 0):
                    pe.wait_ge(x1_ready, NT * 2)
                if what == "km" and g == 0:
                    pe.wait_ge(x1_ready, NT * 3)
                if what == "vm" and g == 0:
                    pe.wait_ge(x1_ready, NT * 4)
                if what == "qm":
                    b = BLOCKS.index(("x1", g, 4))
                    pe.wait_ge(block_lo, 2 * (max(b, BLOCKS.index(("mem", 2, 6))) + 1))
                if what == "wo" and n == 0:
                    pe.wait_ge(omT_ready, NT)
                hi, lo = operand[what]
                for hf in range(2):
                    k0 = (g * GK if what in ("out", "km", "vm") else 0) + hf * (GK // 2)
                    first = (g == 0 and hf == 0) if what != "wo" else hf == 0
                    last = (g == NG - 1 and hf == 1) if what != "wo" else hf == 1
                    half_group(TAIL_HALF0 + 2 * w + hf, hf + 2 * (w % 2), banks_of[what, n], hi, lo, k0, first, last)
                    if 2 * w + hf <= 11:
                        attend(2 * w + hf, PAIRS - 1, MOBA, 11)
                if w in BLOCK_AFTER:
                    transpose_block(BLOCK_AFTER[w])
                if (what, n, g) == ("km", 0, 2):
                    pe.wait_ge(qm_ready, NT)
                    for h in range(4):
                        for t in range(NT):
                            m = pe.transpose(ps[:, 4 + h // 2, ((h % 2) * NT + t) * P:((h % 2) * NT + t + 1) * P],
                                             qm_sb[:, t, h * P:(h + 1) * P], ident[:, :])
                        if h % 2:
                            m.then_inc(qmT_made, 1)
                if (what, n, g) == ("vm", 0, 0):
                    pe.wait_ge(km_ready, NT)
                    for h in range(4):
                        for t in range(NT):
                            m = pe.transpose(ps[:, 6 + h // 2, ((h % 2) * NT + t) * P:((h % 2) * NT + t + 1) * P],
                                             km_sb[:, t, h * P:(h + 1) * P], ident[:, :])
                        if h % 2:
                            m.then_inc(kmT_made, 1)
                if (what, n, g) == ("vm", 0, 1):
                    pe.wait_ge(qmT_ready, 2)
                    pe.wait_ge(kmT_ready, 2)
                    for t in range(NT):
                        for h in range(4):
                            m = pe.matmul(ps[:, (4, 0)[t] + h // 2, (h % 2) * SEQ:(h % 2 + 1) * SEQ],
                                          qmT_sb[:, h, t * P:(t + 1) * P], kmT_sb[:, h, :], start=True, stop=True)
                        m.then_inc(scores_m_made, 1)
                if what == "vm" and g >= 2:
                    t = g - 2
                    pe.wait_ge(exp_m_ready, t + 1)
                    for kb in range(2):
                        for h in range(4):
                            m = pe.transpose(ps[:, (6, 4)[t] + kb, h * P:(h + 1) * P],
                                             pm_sb[:, t, h, kb * P:(kb + 1) * P], ident[:, :])
                        m.then_inc(pmT_made, 1)
                if (what, n, g) == ("vm", 0, 3):
                    pe.wait_ge(vm_ready, NT)
                    for t in range(NT):
                        pe.wait_ge(pmT_ready[0], t + 1)
                        pe.wait_ge(pmT_ready[1], t + 1)
                        for h in range(4):
                            head = slice(h * P, (h + 1) * P)
                            pe.matmul(ps[:, t, head], pmT_sb[:, t, 0, h], vm_sb[:, 0, head], start=True, stop=False)
                            m = pe.matmul(ps[:, t, head], pmT_sb[:, t, 1, h], vm_sb[:, 1, head],
                                          start=False, stop=True)
                        m.then_inc(om_made, 1)
                    for t in range(NT):
                        pe.wait_ge(om_ready, t + 1)
                        for h in range(4):
                            m = pe.transpose(ps[:, 6 + t, h * P:(h + 1) * P], o_sb[:, t, h * P:(h + 1) * P],
                                             ident[:, :])
                        m.then_inc(omT_made, 1)

        @block.scalar
        def _(act):
            def split_hi(half, i, turn):
                g = i // 2
                if i % 2 == 0:
                    act.wait_ge(group_loaded[g % RAW], 32 * (turn + g // RAW + 1))
                wait(act, half_done, half - SPLITS + 1)
                act.activation(w_hi[:, i % SPLITS], w_raw[:, g % RAW, (i % 2) * 2:(i % 2) * 2 + 2],
                               ACT.Copy).then_inc(hi_made, 1)

            def block_hi_bank(b, i):
                source, n, bank = BLOCKS[b]
                first_gain = {"x": 0, "x1": KO, "mem": 2 * KO}[source]
                act.wait_ge(block_made, 2 * b + i + 1)
                for k in (2 * i, 2 * i + 1):
                    into = cT_hi[:, k] if source == "x1" else aT_hi[:, GK * n + k]
                    gain = first_gain + GK * n + k
                    m = act.activation(into, ps[:, bank + i, (k % 2) * SEQ:(k % 2 + 1) * SEQ], ACT.Identity,
                                       scale=gainsT[:, gain:gain + 1])
                m.then_inc(block_hi, 1)

            def chunk_b_out(a, t):
                gate = ps[:, 2 + t, 2 * P:4 * P]
                act.activation(sig_sb[:, t], gate, ACT.Exp, scale=neg_r_x[:, t:t + 1])
                act.activation(gate_sb[:, t], gate, ACT.Identity, scale=r_x[:, t:t + 1]).then_inc(gate_ready, 1)
                m = act.activation(v_sb[:, t], ps[:, 2 + t, 0:2 * P], ACT.Identity, scale=r_x[:, t:t + 1])
                if t == NT - 1:
                    m.then_inc(v_ready, 1)

            def attend(n, a, kind):
                x_bank, y_bank = (6, 4), (7, 5)
                if n == 0:
                    act.wait_ge(half_done, PAIR_HALVES * (a + 1))
                    wait(act, y_ready, a)
                    chunk_b_out(a, 0)
                if n == 1:
                    act.wait_ge(qkT_made, 2 * a + 1)
                    act.activation(qT_sb[:, :, :].rearrange("p u s -> p (u s)"), ps[:, 4, :], ACT.Copy,
                                   scale=kind.scale).then_inc(qT_ready, 1)
                if n == 2:
                    chunk_b_out(a, 1)
                if n in (4, 5):
                    u = n - 4
                    act.wait_ge(max_ready, 2 * a + u + 1)
                    for c in range(kind.maps):
                        for t in (1, 0):
                            cols = slice(0, SEQ) if t == 1 else slice(SEQ, SEQ + P)
                            m = act.activation(prob_sb[:, u, c, cols], prob_sb[:, u, c, cols], ACT.Exp,
                                               bias=neg_max[:, u, t, c:c + 1],
                                               accum_out=exp_sum[:, c, u, t:t + 1])
                    m.then_inc(exp_ready, 1)
                if n in (7, 9):
                    u = (n - 7) // 2
                    act.wait_ge(probT_made, 2 * a + u + 1)
                    act.activation(probT_sb[:, u].rearrange("p i q -> p (i q)"), ps[:, x_bank[u], 0:3 * P],
                                   ACT.Copy).then_inc(probT_ready, 1)
                if n in (8, 10) and kind.diff:
                    u = (n - 8) // 2
                    act.wait_ge(pv_made, 2 * a + u + 1)
                    for t in range(NT):
                        m = act.activation(junk[:, t * P:(t + 1) * P], ps[:, y_bank[u], t * P:(t + 1) * P],
                                           ACT.Square, accum_out=o_sq[:, u, t:t + 1])
                    m.then_inc(o_summed, 1)

            def qk1_out(j):
                act.wait_ge(half_done, PAIR_HALVES * j + PAIR_HALVES // 2)
                act.activation(qk_sb[:, 1], ps[:, 1, :], ACT.Identity, scale=r_x[:, 1:2]).then_inc(qk1_ready, 1)

            def pair_window(j, kind):
                for n in range(PAIR_HALVES):
                    split_hi(PAIR_HALVES * j + n + 2, n + 2, 2 * j)
                    attend(n, j - 1, kind)
                    if n == PAIR_HALVES // 2:
                        qk1_out(j)

            act.dma_start(gains[0:KO, :], norm_mix_g[0].rearrange("(k p) -> k p", p=P)).then_inc(gains_loaded, 16)
            act.dma_start(gains[KO:2 * KO, :], norm_mem_g[0].rearrange("(k p) -> k p", p=P)).then_inc(gains_loaded, 16)
            act.dma_start(gains[2 * KO:3 * KO, :], mem_norm_g[0].rearrange("(k p) -> k p", p=P)
                          ).then_inc(gains_loaded, 16)
            act.dma_start(gains[3 * KO:3 * KO + 1, :], subln_g).then_inc(gains_loaded, 16)
            for i, vec in enumerate((lambda_q1, lambda_k1, lambda_q2, lambda_k2)):
                act.dma_start(lam_in[:, i], vec[0].partition_broadcast(P)).then_inc(lam_loaded, 16)
            act.dma_start(final_gs[:, :], final_g.partition_broadcast(P)).then_inc(final_g_loaded, 16)

            act.wait_ge(gainsT_ready, 1)
            for i in range(4):
                block_hi_bank(i // 2, i % 2)
            split_hi(0, 0, 0)
            split_hi(1, 1, 0)
            for n in range(PAIR_HALVES):
                split_hi(n + 2, n + 2, 0)
                if n in (1, 2):
                    block_hi_bank(n + 1, 0)
                    block_hi_bank(n + 1, 1)
                if n == 3:
                    for q in range(4):
                        act.wait_ge(x_loaded[q], 16)
                if n in (3, 4):
                    act.activation(junk_row, xs[:, n - 3, :], ACT.Square,
                                   accum_out=x_sq[:, n - 3:n - 2]).then_inc(x_summed, 1)
                    act.wait_ge(x_summed, n - 2)
                if n == 7:
                    act.wait_ge(lam_dots, 2)
                    act.activation(lam_exp, lam_dot, ACT.Exp).then_inc(lam_exps, 1)
                if n == PAIR_HALVES // 2:
                    act.wait_ge(r_x_ready, 1)
                    qk1_out(0)
            with act.Fori(1, KIND_PAIRS + 1) as j:
                pair_window(j, DIFF)
            with act.Fori(KIND_PAIRS + 1, PAIRS) as j:
                pair_window(j, MOBA)

            block_half = {2 * w + 2: b for w, b in BLOCK_AFTER.items()}
            for i in range(2 * len(TAIL)):
                if i + 2 < 2 * len(TAIL):
                    split_hi(TAIL_HALF0 + i + 2, i + 2, 2 * PAIRS)
                if i <= 11:
                    attend(i, PAIRS - 1, MOBA)
                if i in block_half:
                    block_hi_bank(block_half[i], 0)
                if i - 1 in block_half:
                    block_hi_bank(block_half[i - 1], 1)
                if i in (17, 19, 27, 39):
                    n = {17: 0, 19: 1, 27: 2, 39: 3}[i]
                    act.wait_ge(x1_ready, NT * (n + 1))
                    for t in range(NT):
                        m = act.activation(junk[:, :], xs[:, t, n * COLS:(n + 1) * COLS], ACT.Square,
                                           accum_out=x1_sq[:, t, n:n + 1])
                        m.then_inc(x1_summed, 1)
                        act.wait_ge(x1_summed, NT * n + t + 1)
                if i in range(28, 36):
                    t, q = (i - 28) // 4, i % 4
                    if i == 28:
                        act.wait_ge(mem_loaded, 16)
                    act.activation(junk[:, :], mems[:, t, q * COLS:(q + 1) * COLS], ACT.Square,
                                   accum_out=mem_sq4[:, t, q:q + 1]).then_inc(mem_summed, 1)
                    act.wait_ge(mem_summed, i - 27)
                if i == 44:
                    act.wait_ge(half_done, done_at("qm", 0, 3))
                    act.wait_ge(q_scale_ready, 1)
                    act.activation(qm_sb[:, 1], ps[:, 7, :], ACT.Identity, scale=q_scale[:, 1:2]
                                   ).then_inc(qm_ready, 1)
                if i == 46:
                    act.wait_ge(qmT_made, 1)
                    act.activation(qmT_sb[:, 0:2].rearrange("p h s -> p (h s)"), ps[:, 4, :], ACT.Copy
                                   ).then_inc(qmT_ready, 1)
                if i == 48:
                    act.wait_ge(half_done, done_at("km", 0, 3))
                    act.wait_ge(r_mem_steps, 2 + RSQRT_STEPS)
                    act.activation(km_sb[:, 1], ps[:, 1, :], ACT.Identity, scale=r_mem[:, 1:2]
                                   ).then_inc(km_ready, 1)
                if i == 50:
                    act.wait_ge(kmT_made, 1)
                    act.activation(kmT_sb[:, 0:2].rearrange("p h s -> p (h s)"), ps[:, 6, :], ACT.Copy
                                   ).then_inc(kmT_ready, 1)
                if i in (53, 54):
                    t = i - 53
                    act.wait_ge(max_m_ready, t + 1)
                    for h in range(4):
                        m = act.activation(pm_sb[:, t, h], ps[:, (4, 0)[t] + h // 2, (h % 2) * SEQ:(h % 2 + 1) * SEQ],
                                           ACT.Exp, bias=neg_max_m[:, t, h:h + 1], accum_out=sum_m[:, t, h:h + 1])
                    m.then_inc(exp_m_ready, 1)
                if i == 55:
                    for t in range(NT):
                        if t == 1:
                            act.wait_ge(half_done, done_at("vm", 0, 3))
                            act.activation(vm_sb[:, 1], ps[:, 3, :], ACT.Identity, scale=r_mem[:, 1:2]
                                           ).then_inc(vm_ready, 1)
                        act.wait_ge(pmT_made, 2 * t + 1)
                        act.activation(pmT_sb[:, t, 0].rearrange("p h q -> p (h q)"), ps[:, (6, 4)[t], :], ACT.Copy
                                       ).then_inc(pmT_ready[0], 1)
                    for t in range(NT):
                        act.wait_ge(omT_made, t + 1)
                        act.activation(cT_hi[:, :, t * P:(t + 1) * P],
                                       ps[:, 6 + t, :].rearrange("p (h q) -> p h q", q=P), ACT.Copy
                                       ).then_inc(omT_hi_ready, 1)
            for n in range(4):
                for t in range(NT):
                    act.wait_ge(x2_ready, NT * n + t + 1)
                    act.activation(junk[:, :], xs[:, t, n * COLS:(n + 1) * COLS], ACT.Square,
                                   accum_out=x2_sq[:, t, n:n + 1]).then_inc(x2_summed, 1)
                    act.wait_ge(x2_summed, NT * n + t + 1)
            act.wait_ge(x2_gained, 4 * NT)
            act.wait_ge(r_x2_steps, 2 + RSQRT_STEPS)
            act.activation(xs[:, 1, :], xs[:, 1, :], ACT.Identity, scale=r_x2[:, 1:2]).then_inc(out_ready[1], 1)

        @block.vector
        def _(dve):
            def split_lo(half, i):
                g = i // 2
                dve.wait_ge(hi_made, half + 1)
                dve.tensor_tensor(w_lo[:, i % SPLITS], w_raw[:, g % RAW, (i % 2) * 2:(i % 2) * 2 + 2],
                                  w_hi[:, i % SPLITS].bitcast(F32), ALU.subtract).then_inc(lo_made, 1)

            def block_lo_bank(b, i):
                source, n, bank = BLOCKS[b]
                first_gain = {"x": 0, "x1": KO, "mem": 2 * KO}[source]
                dve.wait_ge(block_hi, 2 * b + i + 1)
                for k in (2 * i, 2 * i + 1):
                    hi, lo = (cT_hi[:, k], cT_lo[:, k]) if source == "x1" else \
                             (aT_hi[:, GK * n + k], aT_lo[:, GK * n + k])
                    gain = first_gain + GK * n + k
                    m = dve.scalar_tensor_tensor(lo, ps[:, bank + i, (k % 2) * SEQ:(k % 2 + 1) * SEQ],
                                                 gainsT[:, gain:gain + 1], hi.bitcast(F32),
                                                 ALU.mult, ALU.subtract)
                m.then_inc(block_lo, 1)

            def rsqrt(y, a, scratch, steps, done):
                dve.tensor_scalar(y.bitcast(I32), a.bitcast(I32), -0.5, RSQRT_SEED, ALU.mult, ALU.add
                                  ).then_inc(steps, 1)
                for i in range(3):
                    dve.wait_ge(steps, done + 3 * i + 1)
                    dve.scalar_tensor_tensor(scratch, a, -0.5, y, ALU.mult, ALU.mult).then_inc(steps, 1)
                    dve.wait_ge(steps, done + 3 * i + 2)
                    dve.tensor_tensor(scratch, scratch, y, ALU.mult).then_inc(steps, 1)
                    dve.wait_ge(steps, done + 3 * i + 3)
                    dve.scalar_tensor_tensor(y, scratch, 1.5, y, ALU.add, ALU.mult).then_inc(steps, 1)
                dve.wait_ge(steps, done + RSQRT_STEPS)

            def silu_piece(a, i):
                t, half = i // 2, slice((i % 2) * P, (i % 2 + 1) * P)
                dve.wait_ge(gate_ready, 2 * a + t + 1)
                s, gate = sig_sb[:, t, half], gate_sb[:, t, half]
                dve.tensor_scalar(s, s, 1.0, None, ALU.add).then_inc(silu_steps, 1)
                dve.wait_ge(silu_steps, 12 * a + 3 * i + 1)
                dve.reciprocal(s, s).then_inc(silu_steps, 1)
                dve.wait_ge(silu_steps, 12 * a + 3 * i + 2)
                dve.tensor_tensor(gate, gate, s, ALU.mult).then_inc(silu_steps, 1)

            def attend(n, a, kind, y_out_at):
                x_bank, y_bank = (6, 4), (7, 5)
                local = a - kind.first_pair
                if n == 1:
                    dve.wait_ge(qkT_made, 2 * a + 2)
                    dve.tensor_copy(kT_sb[:, :, :].rearrange("p u s -> p (u s)"), ps[:, 5, :]).then_inc(kT_ready, 1)
                if n in (1, 2, 7, 9):
                    silu_piece(a, {1: 0, 2: 1, 7: 2, 9: 3}[n])
                if n in (3, 4):
                    u = n - 3
                    dve.wait_ge(scores_made, 2 * a + u + 1)
                    slope = slopes[:, bass.ds(2 * a + u, 1)]
                    banks = ps[:, x_bank[u]:x_bank[u] + kind.maps, :]
                    for cols, d in ((slice(0, SEQ), slice(0, SEQ)), (slice(SEQ, SEQ + P), slice(P, SEQ))):
                        width = cols.stop - cols.start
                        bias = dist[:, d].unsqueeze(1).to_broadcast([P, kind.maps, width])
                        dve.scalar_tensor_tensor(prob_sb[:, u, 0:kind.maps, cols], bias, slope,
                                                 banks[:, :, cols], ALU.mult, ALU.add).then_inc(logits_ready, 1)
                    for i, (t, cols) in enumerate(((1, slice(0, SEQ)), (0, slice(SEQ, SEQ + P)))):
                        dve.wait_ge(logits_ready, 4 * a + 2 * u + i + 1)
                        m = dve.tensor_reduce(neg_max[:, u, t, 0:kind.maps], prob_sb[:, u, 0:kind.maps, cols],
                                              axis=AX.X, op=ALU.max, negate=True)
                    m.then_inc(max_ready, 1)
                if n in (5, 6) and kind.diff:
                    u = n - 5
                    dve.wait_ge(exp_ready, 2 * a + u + 1)
                    dve.reciprocal(inv_sum1[:, u], exp_sum[:, 1, u]).then_inc(mix_steps, 1)
                    dve.wait_ge(mix_steps, 4 * local + 2 * u + 1)
                    dve.scalar_tensor_tensor(mix[:, u], inv_sum1[:, u], neg_lam[:, 0:1], exp_sum[:, 0, u],
                                             ALU.mult, ALU.mult).then_inc(mix_steps, 1)
                    dve.wait_ge(mix_steps, 4 * local + 2 * u + 2)
                    for t, cols in ((1, slice(0, SEQ)), (0, slice(SEQ, SEQ + P))):
                        m = dve.scalar_tensor_tensor(prob_sb[:, u, 0, cols], prob_sb[:, u, 1, cols],
                                                     mix[:, u, t:t + 1], prob_sb[:, u, 0, cols],
                                                     ALU.mult, ALU.add)
                    m.then_inc(attn_ready, 1)
                if n == 10:
                    steps = y_steps[kind.name]
                    if kind.diff:
                        done = local * (5 + RSQRT_STEPS)
                        dve.wait_ge(o_summed, 2 * local + 2)
                        dve.reciprocal(inv_sum0, exp_sum[:, 0]).then_inc(steps, 1)
                        dve.wait_ge(steps, done + 1)
                        dve.tensor_tensor(inv_sq, inv_sum0, inv_sum0, ALU.mult).then_inc(steps, 1)
                        dve.wait_ge(steps, done + 2)
                        dve.scalar_tensor_tensor(o_ms, o_sq, 1.0 / P, inv_sq, ALU.mult, ALU.mult
                                                 ).then_inc(steps, 1)
                        dve.wait_ge(steps, done + 3)
                        dve.tensor_scalar(o_ms, o_ms, EPS, None, ALU.add).then_inc(steps, 1)
                        dve.wait_ge(steps, done + 4)
                        flat = "p u t -> p (u t)"
                        rsqrt(r_o.rearrange(flat), o_ms.rearrange(flat), newton, steps, done + 4)
                        dve.tensor_tensor(y_scale, r_o, inv_sum0, ALU.mult).then_inc(steps, 1)
                        dve.wait_ge(steps, done + 5 + RSQRT_STEPS)
                    else:
                        dve.wait_ge(pv_made, 2 * a + 2)
                        dve.reciprocal(y_scale, exp_sum[:, 0]).then_inc(steps, 1)
                        dve.wait_ge(steps, local + 1)
                    dve.wait_ge(silu_steps, 12 * a + 12)
                    for u in range(2):
                        for t in range(NT):
                            head = slice(u * P, (u + 1) * P)
                            m = dve.scalar_tensor_tensor(y_sb[:, t, head], ps[:, y_bank[u], t * P:(t + 1) * P],
                                                         y_scale[:, u, t:t + 1], gate_sb[:, t, head],
                                                         ALU.mult, ALU.mult)
                    m.then_inc(y_ready, 1)
                if n == y_out_at:
                    gain = sub_gain[:, 0:1] if kind.diff else 1.0
                    hi = yT_hi[:, bass.ds(2 * a, 2), :]
                    lo = yT_lo[:, bass.ds(2 * a, 2), :]
                    yT = ps[:, 6, :].rearrange("p (u s) -> p u s", s=SEQ)
                    dve.wait_ge(yT_made, a + 1)
                    dve.tensor_scalar(hi, yT, gain, None, ALU.mult).then_inc(yT_hi_ready, 1)
                    dve.wait_ge(yT_hi_ready, a + 1)
                    dve.scalar_tensor_tensor(lo, yT, gain, hi.bitcast(F32), ALU.mult, ALU.subtract
                                             ).then_inc(yT_ready, 1)

            def qk0_out(j):
                dve.wait_ge(half_done, PAIR_HALVES * j + PAIR_HALVES // 2)
                dve.tensor_scalar(qk_sb[:, 0], ps[:, 0, :], r_x[:, 0:1], None, ALU.mult).then_inc(qk0_ready, 1)

            def pair_window(j, kind):
                for n in range(PAIR_HALVES):
                    split_lo(PAIR_HALVES * j + n + 2, n + 2)
                    attend(n, j - 1, kind, 14)
                    if n == PAIR_HALVES // 2:
                        qk0_out(j)

            def row_rms(sums, ms, r, steps, extra):
                dve.tensor_scalar(ms, sums, 1.0 / DM, EPS, ALU.mult, ALU.add).then_inc(steps, 1)
                dve.wait_ge(steps, extra + 1)
                rsqrt(r, ms, newton[:, 0:NT], steps, extra + 1)

            dve.wait_ge(gainsT_made, 1)
            dve.tensor_copy(gainsT[:, :], ps[:, 3, 0:3 * KO + 1]).then_inc(gainsT_ready, 1)
            dve.wait_ge(gainsT_ready, 1)
            dve.tensor_scalar(sub_gain, gainsT[:, 3 * KO:3 * KO + 1], 1.0 - LAM_INIT, None, ALU.mult
                              ).then_inc(gainsT_ready, 1)
            dve.wait_ge(gainsT_ready, 2)
            for i in range(4):
                block_lo_bank(i // 2, i % 2)
            split_lo(0, 0)
            split_lo(1, 1)
            for n in range(PAIR_HALVES):
                split_lo(n + 2, n + 2)
                if n in (1, 2):
                    block_lo_bank(n + 1, 0)
                    block_lo_bank(n + 1, 1)
                if n == 5:
                    dve.wait_ge(x_summed, NT)
                    row_rms(x_sq, x_ms, r_x, r_x_steps, 0)
                    dve.tensor_scalar(neg_r_x, r_x, -1.0, None, ALU.mult).then_inc(r_x_ready, 1)
                if n == 6:
                    dve.wait_ge(lam_loaded, 64)
                    for i in range(2):
                        dve.tensor_tensor(lam_prod[:, i], lam_in[:, 2 * i], lam_in[:, 2 * i + 1], ALU.mult
                                          ).then_inc(lam_steps, 1)
                    for i in range(2):
                        dve.wait_ge(lam_steps, i + 1)
                        dve.tensor_reduce(lam_dot[:, i:i + 1], lam_prod[:, i], axis=AX.X, op=ALU.add
                                          ).then_inc(lam_dots, 1)
                if n == PAIR_HALVES // 2:
                    qk0_out(0)
                if n == 9:
                    dve.wait_ge(lam_exps, 1)
                    dve.tensor_tensor(neg_lam, lam_exp[:, 1:2], lam_exp[:, 0:1], ALU.subtract).then_inc(lam_ready, 1)
                    dve.wait_ge(lam_ready, 1)
                    dve.tensor_scalar(neg_lam, neg_lam, -LAM_INIT, None, ALU.add).then_inc(lam_ready, 1)
                    dve.wait_ge(lam_ready, 2)
                    dve.wait_ge(consts_ready, CONSTS)
            with dve.Fori(1, KIND_PAIRS + 1) as j:
                pair_window(j, DIFF)
            with dve.Fori(KIND_PAIRS + 1, PAIRS) as j:
                pair_window(j, MOBA)

            block_half = {2 * w + 2: b for w, b in BLOCK_AFTER.items()}
            for i in range(2 * len(TAIL)):
                if i + 2 < 2 * len(TAIL):
                    split_lo(TAIL_HALF0 + i + 2, i + 2)
                if i <= 12:
                    attend(i, PAIRS - 1, MOBA, 12)
                if i in block_half:
                    block_lo_bank(block_half[i], 0)
                if i - 1 in block_half:
                    block_lo_bank(block_half[i - 1], 1)
                if i in (14, 16, 26, 38):
                    n = {14: 0, 16: 1, 26: 2, 38: 3}[i]
                    dve.wait_ge(half_done, done_at("out", n, 3))
                    for t in range(NT):
                        cols = slice(n * COLS, (n + 1) * COLS)
                        dve.tensor_tensor(xs[:, t, cols], xs[:, t, cols], ps[:, 2 * (n % 2) + t, :], ALU.add
                                          ).then_inc(x1_ready, 1)
                if i == 36:
                    dve.wait_ge(mem_summed, 8)
                    dve.tensor_reduce(mem_sq, mem_sq4, axis=AX.X, op=ALU.add).then_inc(r_mem_steps, 1)
                    dve.wait_ge(r_mem_steps, 1)
                    row_rms(mem_sq, mem_ms, r_mem, r_mem_steps, 1)
                if i == 42:
                    dve.wait_ge(x1_summed, 4 * NT)
                    dve.tensor_reduce(x1_tot, x1_sq, axis=AX.X, op=ALU.add).then_inc(r_x1_steps, 1)
                    dve.wait_ge(r_x1_steps, 1)
                    row_rms(x1_tot, x1_ms, r_x1, r_x1_steps, 1)
                    dve.tensor_scalar(q_scale, r_x1, HEAD_SCALE, None, ALU.mult).then_inc(q_scale_ready, 1)
                    dve.wait_ge(q_scale_ready, 1)
                if i == 44:
                    dve.wait_ge(half_done, done_at("qm", 0, 3))
                    dve.tensor_scalar(qm_sb[:, 0], ps[:, 6, :], q_scale[:, 0:1], None, ALU.mult).then_inc(qm_ready, 1)
                if i == 46:
                    dve.wait_ge(qmT_made, 2)
                    dve.tensor_copy(qmT_sb[:, 2:4].rearrange("p h s -> p (h s)"), ps[:, 5, :]).then_inc(qmT_ready, 1)
                if i == 48:
                    dve.wait_ge(half_done, done_at("km", 0, 3))
                    dve.tensor_scalar(km_sb[:, 0], ps[:, 0, :], r_mem[:, 0:1], None, ALU.mult).then_inc(km_ready, 1)
                if i == 50:
                    dve.wait_ge(kmT_made, 2)
                    dve.tensor_copy(kmT_sb[:, 2:4].rearrange("p h s -> p (h s)"), ps[:, 7, :]).then_inc(kmT_ready, 1)
                if i == 52:
                    for t in range(NT):
                        dve.wait_ge(scores_m_made, t + 1)
                        banks = ps[:, (4, 0)[t]:(4, 0)[t] + 2, :].rearrange("p b (h k) -> p (b h) k", k=SEQ)
                        dve.tensor_reduce(neg_max_m[:, t], banks, axis=AX.X, op=ALU.max, negate=True
                                          ).then_inc(max_m_ready, 1)
                if i == 55:
                    for t in range(NT):
                        if t == 1:
                            dve.wait_ge(half_done, done_at("vm", 0, 3))
                            dve.tensor_scalar(vm_sb[:, 0], ps[:, 2, :], r_mem[:, 0:1], None, ALU.mult
                                              ).then_inc(vm_ready, 1)
                        dve.wait_ge(pmT_made, 2 * t + 2)
                        dve.tensor_copy(pmT_sb[:, t, 1].rearrange("p h q -> p (h q)"), ps[:, (6, 4)[t] + 1, :]
                                        ).then_inc(pmT_ready[1], 1)
                    dve.wait_ge(exp_m_ready, NT)
                    dve.reciprocal(inv_sum_m, sum_m).then_inc(inv_m_ready, 1)
                    dve.wait_ge(inv_m_ready, 1)
                    for t in range(NT):
                        dve.wait_ge(om_made, t + 1)
                        dve.tensor_tensor(o_sb[:, t].rearrange("p (h d) -> p h d", d=P),
                                          ps[:, t, :].rearrange("p (h d) -> p h d", d=P),
                                          inv_sum_m[:, t].unsqueeze(2).to_broadcast([P, 4, P]), ALU.mult
                                          ).then_inc(om_ready, 1)
                    for t in range(NT):
                        dve.wait_ge(omT_hi_ready, t + 1)
                        tok = slice(t * P, (t + 1) * P)
                        dve.tensor_tensor(cT_lo[:, :, tok], ps[:, 6 + t, :].rearrange("p (h q) -> p h q", q=P),
                                          cT_hi[:, :, tok].bitcast(F32), ALU.subtract).then_inc(omT_ready, 1)
            banks_of_wo = {0: 2, 1: 0, 2: 4, 3: 6}
            dve.wait_ge(final_g_loaded, 16)
            for n in range(4):
                dve.wait_ge(half_done, done_at("wo", n, 0))
                cols = slice(n * COLS, (n + 1) * COLS)
                for t in range(NT):
                    dve.tensor_tensor(xs[:, t, cols], xs[:, t, cols], ps[:, banks_of_wo[n] + t, :], ALU.add
                                      ).then_inc(x2_ready, 1)
                for t in range(NT):
                    dve.wait_ge(x2_summed, NT * n + t + 1)
                    dve.tensor_tensor(xs[:, t, cols], xs[:, t, cols], final_gs[:, cols], ALU.mult
                                      ).then_inc(x2_gained, 1)
            dve.tensor_reduce(x2_tot, x2_sq, axis=AX.X, op=ALU.add).then_inc(r_x2_steps, 1)
            dve.wait_ge(r_x2_steps, 1)
            row_rms(x2_tot, x2_ms, r_x2, r_x2_steps, 1)
            dve.wait_ge(x2_gained, 4 * NT)
            dve.tensor_scalar(xs[:, 0, :], xs[:, 0, :], r_x2[:, 0:1], None, ALU.mult).then_inc(out_ready[0], 1)


_INS = ["x", "mem", "norm_mix_g", "w_in", "lambda_q1", "lambda_k1", "lambda_q2", "lambda_k2",
        "subln_g", "w_out", "norm_mem_g", "mem_norm_g", "w_q_mem", "w_kv_mem", "w_o_mem", "final_g"]


def kernel(**inputs):
    import numpy as np
    import concourse.bacc as bacc
    from concourse.bass_utils import run_bass_kernel_spmd as run

    nc = bacc.Bacc("TRN2", target_bir_lowering=False, num_devices=1)
    arrays, args = {}, []
    for name in _INS:
        a = np.ascontiguousarray(inputs[name])
        arrays[f"in_{name}"] = a
        args.append(nc.dram_tensor(f"in_{name}", a.shape, mybir.dt.from_np(a.dtype), kind="ExternalInput").ap())
    out = nc.dram_tensor("out", (1, SEQ, DM), F32, kind="ExternalOutput").ap()
    program(nc, *args, out)
    r = run(nc, [arrays], core_ids=[0])
    return r.results[0]["out"]
```

```python
from contextlib import ExitStack

import concourse.bass as bass
from concourse import mybir

F32 = mybir.dt.float32
F32R = mybir.dt.float32r
I32 = mybir.dt.int32
ACT = mybir.ActivationFunctionType
ALU = mybir.AluOpType
AX = mybir.AxisListType

P = 128
SEQ = 256
DM = 2048
NT = SEQ // P
KO = DM // P
COLS = 512
GK = 4
NG = KO // GK
HEADS = 8
PAIRS = 2 * HEADS // 2
KIND_PAIRS = HEADS // 2
HALF_D = P // 2
PAIR_HALVES = 4 * NG
SPLITS = 4
RAW = 8
EPS = 1e-6
LAM_INIT = 0.2
MASKED = -3.0e38
DIFF_SCALE = float(HALF_D) ** -0.5
HEAD_SCALE = float(P) ** -0.5
RSQRT_SEED = float(0x5F3759DF)
RSQRT_STEPS = 10


class Kind:

    def __init__(self, name, maps, scale, first_pair):
        self.name, self.maps, self.scale, self.first_pair = name, maps, scale, first_pair
        self.diff = maps == 2


DIFF = Kind("diff", 2, DIFF_SCALE, 0)
MOBA = Kind("moba", 1, HEAD_SCALE, KIND_PAIRS)

TAIL = ([("out", 0, g) for g in range(3)] + [("out", 1, g) for g in range(3)]
        + [("out", 0, 3), ("out", 1, 3), ("out", 2, 0), ("out", 2, 1), ("out", 2, 2), ("qm", 0, 0),
           ("out", 2, 3), ("qm", 0, 1), ("out", 3, 0), ("out", 3, 1), ("qm", 0, 2), ("out", 3, 2),
           ("out", 3, 3), ("km", 0, 0), ("km", 0, 1), ("qm", 0, 3), ("km", 0, 2), ("km", 0, 3)]
        + [("vm", 0, g) for g in range(4)])
WO_HALF0 = 2 * len(TAIL)
TAIL_GROUP0 = PAIRS * 2 * NG
TAIL_HALF0 = 2 * TAIL_GROUP0
STREAM = [(what, n, g, hf) for what, n, g in TAIL for hf in range(2)] + [
    ("wo", n, 0, hf) for n in range(4) for hf in range(2)]

BLOCKS = ([("x", 0, 4), ("x", 1, 6), ("x", 2, 4), ("x", 3, 6)]
          + [("mem", 0, 4), ("mem", 1, 6), ("x1", 0, 4), ("mem", 2, 6), ("mem", 3, 4),
             ("x1", 1, 4), ("x1", 2, 4), ("x1", 3, 4)])
BLOCK_AFTER = {5: 4, 6: 5, 8: 6, 9: 7, 10: 8, 11: 9, 14: 10, 19: 11}


WO_PIECES = (((0, 512, 2), (512, 512, 3), (1024, 512, 4), (1536, 512, 5)),
             ((0, 512, 0), (512, 512, 1), (1024, 512, 6), (1536, 256, 7), (1792, 256, 2)))
X_PARTS = ((0, 256), (256, 512), (512, 1024), (1024, 1536), (1536, 2048))
WARM_UP = (5, 4, 2)


def done_at(what, n, g):
    return TAIL_HALF0 + 2 * (TAIL.index((what, n, g)) + 1)


def wait(engine, semaphore, value):
    if isinstance(value, int) and value <= 0:
        return
    engine.wait_ge(semaphore, value)


def program(nc, x, mem, norm_mix_g, w_in, lambda_q1, lambda_k1, lambda_q2, lambda_k2,
            subln_g, w_out, norm_mem_g, mem_norm_g, w_q_mem, w_kv_mem, w_o_mem, final_g, out):
    with ExitStack() as ctx:
        def sbuf(name, shape, dtype=F32):
            return ctx.enter_context(nc.sbuf_tensor(name, shape, dtype))

        def sem(name):
            return ctx.enter_context(nc.semaphore(name))

        w_raw = sbuf("w_raw", [P, RAW, GK // 2, COLS])
        w_hi = sbuf("w_hi", [P, SPLITS, GK // 2, COLS], F32R)
        w_lo = sbuf("w_lo", [P, SPLITS, GK // 2, COLS], F32R)
        aT_hi = sbuf("aT_hi", [P, KO, SEQ], F32R)
        aT_lo = sbuf("aT_lo", [P, KO, SEQ], F32R)
        yT_hi = sbuf("yT_hi", [P, KO, SEQ], F32R)
        yT_lo = sbuf("yT_lo", [P, KO, SEQ], F32R)
        cT_hi = sbuf("cT_hi", [P, GK, SEQ], F32R)
        cT_lo = sbuf("cT_lo", [P, GK, SEQ], F32R)
        xs = sbuf("xs", [P, NT, DM])
        mems = sbuf("mems", [P, NT, DM])
        qT_hi = sbuf("qT_hi", [P, 2, SEQ], F32R)
        qT_lo = sbuf("qT_lo", [P, 2, SEQ], F32R)
        kT_parts = sbuf("kT_parts", [P, 2, 2, SEQ], F32R)
        v_parts = sbuf("v_parts", [P, NT, 2, 2 * P], F32R)
        probT_hi = sbuf("probT_hi", [P, 2, 3, P], F32R)
        probT_lo = sbuf("probT_lo", [P, 2, 3, P], F32R)
        pool = sbuf("pool", [P, 9 * COLS])
        ident = sbuf("ident", [P, P])
        dist = sbuf("dist", [P, SEQ])
        slopes = sbuf("slopes", [P, 2 * HEADS])
        mix_gain = sbuf("mix_gain", [KO, P])
        gains = sbuf("gains", [2 * KO + 1, P])
        gainsT = sbuf("gainsT", [P, 3 * KO + 1])
        small = sbuf("small", [P, 160])
        wo_hi = yT_hi[:, :, :].rearrange("p k s -> p (k s)").rearrange("p (h k n) -> p h k n", k=GK // 2, n=COLS)
        wo_lo = yT_lo[:, :, :].rearrange("p k s -> p (k s)").rearrange("p (h k n) -> p h k n", k=GK // 2, n=COLS)
        final_gs = w_raw[:, 0:2].rearrange("p h k n -> p (h k n)")

        def carve(tensor, start, *shape):
            size = 1
            for s in shape:
                size *= s
            flat = tensor[:, start:start + size]
            if len(shape) == 1:
                return flat, start + size
            names = "abcd"[:len(shape)]
            view = flat.rearrange(f"p ({' '.join(names)}) -> p {' '.join(names)}",
                                  **{n: s for n, s in zip(names, shape)})
            return view, start + size

        qk_sb, at = carve(pool, 0, NT, COLS)
        gate_sb, at = carve(pool, at, NT, 2 * P)
        sig_sb, at = carve(pool, at, NT, 2 * P)
        prob_sb, at = carve(pool, at, 2, 2, SEQ + P)
        y_sb, at = carve(pool, at, NT, 2 * P)
        junk, at = carve(pool, at, COLS)
        assert at <= 9 * COLS
        junk_row, _ = carve(pool, 0, DM)
        lam_in, _ = carve(pool, DM, 4, HALF_D)
        lam_prod, _ = carve(pool, DM + 4 * HALF_D, 2, HALF_D)
        qm_sb, at = carve(pool, 0, NT, COLS)
        km_sb, at = carve(pool, at, NT, COLS)
        vm_sb = km_sb
        qmT_sb, at = carve(pool, at, 4, SEQ)
        kmT_sb, at = carve(pool, at, 4, SEQ)
        assert at <= 8 * COLS
        mem_flat = mems[:, :, :].rearrange("p t d -> p (t d)")
        pm_sb, at = carve(mem_flat, 0, NT, 4, SEQ)
        pmT_sb, at = carve(mem_flat, at, NT, 2, 4, P)
        result = mems

        def columns(start, *shape):
            return carve(small, start, *shape)

        x_sq, at = columns(0, NT)
        x_ms, at = columns(at, NT)
        r_x, at = columns(at, NT)
        neg_r_x, at = columns(at, NT)
        newton, at = columns(at, 4)
        neg_max, at = columns(at, 2, 2, 2)
        exp_sum, at = columns(at, 2, 2, 2)
        inv_sum1, at = columns(at, 2, 2)
        mix, at = columns(at, 2, 2)
        inv_sum0, at = columns(at, 2, 2)
        inv_sq, at = columns(at, 2, 2)
        o_sq, at = columns(at, 2, 2)
        o_ms, at = columns(at, 2, 2)
        r_o, at = columns(at, 2, 2)
        y_scale, at = columns(at, 2, 2)
        lam_dot, at = columns(at, 2)
        lam_exp, at = columns(at, 2)
        neg_lam, at = columns(at, 1)
        mem_sq4, at = columns(at, NT, 4)
        mem_sq, at = columns(at, NT)
        sub_gain, at = columns(at, 1)
        warm, at = columns(at, 1)
        x1_tot, at = columns(at, NT)
        x2_tot, at = columns(at, NT)
        mem_ms, at = columns(at, NT)
        r_mem, at = columns(at, NT)
        x1_sq, at = columns(at, NT, 4)
        x1_ms, at = columns(at, NT)
        r_x1, at = columns(at, NT)
        q_scale, at = columns(at, NT)
        neg_max_m, at = columns(at, NT, 4)
        sum_m, at = columns(at, NT, 4)
        inv_sum_m, at = columns(at, NT, 4)
        x2_sq, at = columns(at, NT, 5)
        x2_base, at = columns(at, NT)
        x2_ms, at = columns(at, NT)
        x2_half, at = columns(at, NT)
        r_x2, at = columns(at, NT)
        assert at <= 160

        ps = ctx.enter_context(nc.psum_tensor("ps", [P, 8, COLS], F32))

        x_loaded = [sem(f"x_loaded{n}") for n in range(len(X_PARTS))]
        mem_loaded = sem("mem_loaded")
        mix_gain_loaded = sem("mix_gain_loaded")
        gains_loaded = sem("gains_loaded")
        warm_ready = sem("warm_ready")
        lam_loaded = sem("lam_loaded")
        final_g_loaded = sem("final_g_loaded")
        half_loaded = [sem(f"half_loaded{s}") for s in range(RAW)]
        first_hi = sem("first_hi")
        first_lo = sem("first_lo")
        hi_made = sem("hi_made")
        lo_made = sem("lo_made")
        half_done = sem("half_done")
        ident_ready = sem("ident_ready")
        consts_ready = sem("consts_ready")
        gainsT_made = sem("gainsT_made")
        gainsT_ready = sem("gainsT_ready")
        block_made = sem("block_made")
        block_hi = sem("block_hi")
        block_lo = sem("block_lo")
        x_summed = sem("x_summed")
        r_x_steps = sem("r_x_steps")
        r_x_ready = sem("r_x_ready")
        lam_steps = sem("lam_steps")
        lam_dots = sem("lam_dots")
        lam_exps = sem("lam_exps")
        lam_ready = sem("lam_ready")
        qk0_ready = sem("qk0_ready")
        qk1_ready = sem("qk1_ready")
        gate_ready = sem("gate_ready")
        v_hi_ready = sem("v_hi_ready")
        v_ready = sem("v_ready")
        silu_steps = sem("silu_steps")
        qkT_made = sem("qkT_made")
        qkT_hi_ready = sem("qkT_hi_ready")
        qkT_ready = sem("qkT_ready")
        scores_made = sem("scores_made")
        logits_ready = sem("logits_ready")
        max_ready = sem("max_ready")
        exp_ready = sem("exp_ready")
        mix_steps = sem("mix_steps")
        attn_ready = sem("attn_ready")
        probT_made = sem("probT_made")
        probT_hi_ready = sem("probT_hi_ready")
        probT_ready = sem("probT_ready")
        pv_made = sem("pv_made")
        o_ready = sem("o_ready")
        o_summed = sem("o_summed")
        y_steps = {"diff": sem("y_steps_diff"), "moba": sem("y_steps_moba")}
        y_ready = sem("y_ready")
        yT_made = sem("yT_made")
        yT_hi_ready = sem("yT_hi_ready")
        yT_ready = sem("yT_ready")
        mem_summed = sem("mem_summed")
        r_mem_steps = sem("r_mem_steps")
        x1_ready = sem("x1_ready")
        x1_summed = sem("x1_summed")
        r_x1_steps = sem("r_x1_steps")
        q_scale_ready = sem("q_scale_ready")
        qm_ready = sem("qm_ready")
        qmT_made = sem("qmT_made")
        qmT_ready = sem("qmT_ready")
        km_ready = sem("km_ready")
        kmT_made = sem("kmT_made")
        kmT_ready = sem("kmT_ready")
        vm_ready = sem("vm_ready")
        scores_m_made = sem("scores_m_made")
        max_m_ready = sem("max_m_ready")
        exp_m_ready = sem("exp_m_ready")
        inv_m_ready = sem("inv_m_ready")
        pmT_made = sem("pmT_made")
        pmT_ready = [sem("pmT_ready_act"), sem("pmT_ready_dve")]
        pm_ready = sem("pm_ready")
        omT_made = sem("omT_made")
        omT_hi_ready = sem("omT_hi_ready")
        omT_ready = sem("omT_ready")
        wo_done = sem("wo_done")
        x2_ready = sem("x2_ready")
        x2_summed = sem("x2_summed")
        x2_gained = sem("x2_gained")
        r_x2_steps = sem("r_x2_steps")
        r_x2_ready = sem("r_x2_ready")
        out_ready = [sem("out_ready_dve"), sem("out_ready_act")]
        out_stored = sem("out_stored")

        rows = "(h k p) n -> h p k n"
        in_slabs = w_in[0].rearrange("(h k p) (s c) -> h p k s c", k=GK // 2, p=P, c=HEADS * P)
        tail_groups = {"out": w_out[0].rearrange(rows, k=GK // 2, p=P),
                       "qm": w_q_mem[0].rearrange(rows, k=GK // 2, p=P),
                       "km": w_kv_mem[0].rearrange(rows, k=GK // 2, p=P),
                       "vm": w_kv_mem[0].rearrange(rows, k=GK // 2, p=P),
                       "wo": w_o_mem[0].rearrange(rows, k=GK // 2, p=P)}
        x_tiles = x[0].rearrange("(t p) d -> p t d", p=P)
        mem_tiles = mem[0].rearrange("(t p) d -> p t d", p=P)
        out_tiles = out[0].rearrange("(t p) d -> p t d", p=P)

        block = ctx.enter_context(nc.Block())

        @block.sync
        def _(sp):
            SLABS = {("diff", 0): (0, 1), ("diff", 1): (2, 6), ("moba", 0): (3, 4), ("moba", 1): (5, 7)}

            def load_pair_half(kind, pair, local, n):
                wait(sp, lo_made, PAIR_HALVES * pair + n - RAW + 1)
                for part, slab in enumerate(SLABS[kind.name, n // (2 * NG)]):
                    sp.dma_start(w_raw[:, n % RAW, :, part * 2 * P:(part + 1) * 2 * P],
                                 in_slabs[n % (2 * NG)][:, :, slab, bass.ds(2 * P * local, 2 * P)]
                                 ).then_inc(half_loaded[n % RAW], 16)

            def load_x(n):
                a, b = X_PARTS[n]
                sp.dma_start(xs[:, :, a:b], x_tiles[:, :, a:b]).then_inc(x_loaded[n], 16)

            load_x(0)
            for n in range(PAIR_HALVES):
                load_pair_half(DIFF, 0, 0, n)
                if n in (0, 1, 3, 5):
                    load_x((n + 1) // 2 + 1)
                if n == 5:
                    for row, vec in ((0, norm_mem_g), (KO, mem_norm_g)):
                        sp.dma_start(gains[row:row + KO, :], vec[0].rearrange("(k p) -> k p", p=P)
                                     ).then_inc(gains_loaded, 16)
                    sp.dma_start(gains[2 * KO:2 * KO + 1, :], subln_g).then_inc(gains_loaded, 16)
                if n == PAIR_HALVES // 2:
                    for i, vec in enumerate((lambda_q1, lambda_k1, lambda_q2, lambda_k2)):
                        sp.dma_start(lam_in[:, i], vec[0].partition_broadcast(P)).then_inc(lam_loaded, 16)
            with sp.Fori(1, KIND_PAIRS) as j:
                for n in range(PAIR_HALVES):
                    load_pair_half(DIFF, j, j, n)
            with sp.Fori(KIND_PAIRS, PAIRS) as j:
                for n in range(PAIR_HALVES):
                    load_pair_half(MOBA, j, j - KIND_PAIRS, n)
            sp.dma_start(mems[:, :, :], mem_tiles).then_inc(mem_loaded, 16)
            for i, (what, n, g, hf) in enumerate(STREAM):
                first_col = n * COLS + (COLS if what == "vm" else 0)
                sp.wait_ge(lo_made, TAIL_HALF0 + i - RAW + 1)
                for k in range(GK // 2):
                    sp.dma_start(w_raw[:, i % RAW, k], tail_groups[what][2 * g + hf][:, k, first_col:first_col + COLS]
                                 ).then_inc(half_loaded[i % RAW], 16)
            sp.wait_ge(lo_made, TAIL_HALF0 + WO_HALF0 + 2)
            sp.dma_start(final_gs, final_g.partition_broadcast(P)).then_inc(final_g_loaded, 16)
            sp.wait_ge(out_ready[0], 1)
            sp.dma_start(out_tiles[:, 0, :], result[:, 0, :]).then_inc(out_stored, 16)
            for i, (q, engine) in enumerate(((0, 0), (2, 1), (1, 0), (3, 1))):
                sp.wait_ge(out_ready[engine], (2, 1, 3, 2)[i])
                cols = slice(q * COLS, (q + 1) * COLS)
                sp.dma_start(out_tiles[:, 1, cols], result[:, 1, cols]).then_inc(out_stored, 16)
            sp.wait_ge(out_stored, 16 * 5)

        @block.gpsimd
        def _(pool_e):
            pool_e.memset(ident[:, :], 0.0).then_inc(ident_ready, 1)
            pool_e.memset(warm, 0.0).then_inc(warm_ready, 1)
            pool_e.iota(dist[:, :], pattern=[[1, SEQ]], base=-P, channel_multiplier=-1,
                        allow_small_or_imprecise_dtypes=True).then_inc(consts_ready, 1)
            pool_e.wait_ge(ident_ready, 1)
            pool_e.affine_select(out=ident[:, :], in_=ident[:, :], compare_op=ALU.not_equal, fill=1.0,
                                 base=0, pattern=[[-1, P]], channel_multiplier=1).then_inc(ident_ready, 1)
            pool_e.wait_ge(consts_ready, 1)
            pool_e.affine_select(out=dist[:, :], in_=dist[:, :], compare_op=ALU.is_ge, fill=MASKED,
                                 base=P, pattern=[[-1, SEQ]], channel_multiplier=1).then_inc(consts_ready, 1)
            for h in range(HEADS):
                for kind in range(2):
                    pool_e.memset(slopes[:, kind * HEADS + h:kind * HEADS + h + 1],
                                  2.0 ** (-8.0 * (h + 1) / HEADS)).then_inc(consts_ready, 1)

        CONSTS = 2 + 2 * HEADS

        @block.tensor
        def _(pe):
            def half_group(half, slot, banks, hi, lo, k0, first, last):
                first_half = isinstance(half, int) and half == 0
                if first_half:
                    pe.wait_ge(first_lo, 1)
                else:
                    wait(pe, lo_made, half + 1)
                for k in range(GK // 2):
                    if first_half and k == 1:
                        pe.wait_ge(lo_made, 1)
                    for t in range(NT):
                        tok = slice(t * P, (t + 1) * P)
                        acc = ps[:, banks[t], :]
                        pe.matmul(acc, hi[:, k0 + k, tok], w_hi[:, slot, k], start=first and k == 0, stop=False)
                        pe.matmul(acc, hi[:, k0 + k, tok], w_lo[:, slot, k], start=False, stop=False)
                        m = pe.matmul(acc, lo[:, k0 + k, tok], w_hi[:, slot, k], start=False,
                                      stop=last and k == GK // 2 - 1)
                m.then_inc(half_done, 1)

            def keep_busy(count):
                with pe.Fori(0, count):
                    pe.matmul(ps[:, 2, 0:P], ident[:, :], ident[:, :], start=True, stop=True)

            def transpose_block(b):
                source, n, bank = BLOCKS[b]
                rows_of = {"x": xs, "mem": mems, "x1": xs}[source]
                before = [c for c in range(b) if BLOCKS[c][2] == bank]
                if source == "x" and n > 0:
                    pe.wait_ge(x_loaded[n + 1], 16)
                if source == "mem":
                    pe.wait_ge(mem_loaded, 16)
                if source == "x1":
                    pe.wait_ge(x1_ready, NT * (n + 1))
                if before:
                    pe.wait_ge(block_lo, 2 * (before[-1] + 1))
                for i in range(2):
                    if source == "x" and n == 0:
                        pe.wait_ge(x_loaded[i], 16)
                    for k in range(2):
                        for t in range(NT):
                            col = n * COLS + (2 * i + k) * P
                            m = pe.transpose(ps[:, bank + i, (k * NT + t) * P:(k * NT + t + 1) * P],
                                             rows_of[:, t, col:col + P], ident[:, :])
                    m.then_inc(block_made, 1)
                    if source == "x" and n == 0:
                        keep_busy(WARM_UP[1 + i])

            def attend(n, a, kind, yT_after):
                x_bank, y_bank = (6, 4), (7, 5)
                if n == 0:
                    for part in range(2):
                        for u in range(2):
                            for t in range(NT):
                                col = (part * 2 + u) * P
                                m = pe.transpose(ps[:, 4 + part, (u * NT + t) * P:(u * NT + t + 1) * P],
                                                 qk_sb[:, t, col:col + P], ident[:, :])
                        m.then_inc(qkT_made, 1)
                if n in (2, 3):
                    u = n - 2
                    if u == 0:
                        pe.wait_ge(qkT_ready, 2 * a + 2)
                    banks = (x_bank[u], y_bank[u])
                    for c in range(kind.maps):
                        part = slice(c * HALF_D, (c + 1) * HALF_D) if kind.diff else slice(0, P)
                        acc = ps[:, banks[c], 0:SEQ]
                        pe.matmul(acc, qT_hi[part, u, P:SEQ], kT_parts[part, u, 0], start=True, stop=False)
                        pe.matmul(acc, qT_hi[part, u, P:SEQ], kT_parts[part, u, 1], start=False, stop=False)
                        pe.matmul(acc, qT_lo[part, u, P:SEQ], kT_parts[part, u, 0], start=False, stop=True)
                    for c in range(kind.maps):
                        part = slice(c * HALF_D, (c + 1) * HALF_D) if kind.diff else slice(0, P)
                        acc = ps[:, banks[c], SEQ:2 * SEQ]
                        pe.matmul(acc, qT_hi[part, u, 0:P], kT_parts[part, u, :, 0:P], start=True, stop=False)
                        m = pe.matmul(acc[:, P:2 * P], qT_lo[part, u, 0:P], kT_parts[part, u, 0, 0:P],
                                      start=False, stop=True)
                    m.then_inc(scores_made, 1)
                if n in (6, 8):
                    u = (n - 6) // 2
                    pe.wait_ge(attn_ready if kind.diff else exp_ready, 2 * a + u + 1)
                    for i, col in enumerate((SEQ, 0, P)):
                        m = pe.transpose(ps[:, x_bank[u], i * P:(i + 1) * P], prob_sb[:, u, 0, col:col + P],
                                         ident[:, :])
                    m.then_inc(probT_made, 1)
                if n in (8, 10):
                    u = (n - 8) // 2
                    pe.wait_ge(probT_ready, 2 * a + u + 1)
                    if u == 0:
                        pe.wait_ge(v_ready, 2 * a + 2)
                    head = slice(u * P, (u + 1) * P)
                    for t, i, kt in ((0, 0, 0), (1, 1, 0), (1, 2, 1)):
                        acc = ps[:, y_bank[u], 2 * t * P:2 * (t + 1) * P]
                        pe.matmul(acc, probT_hi[:, u, i], v_parts[:, kt, :, head], start=kt == 0, stop=False)
                        m = pe.matmul(acc[:, P:2 * P], probT_lo[:, u, i], v_parts[:, kt, 0, head],
                                      start=False, stop=kt == t)
                    m.then_inc(pv_made, 1)
                if n == yT_after:
                    pe.wait_ge(y_ready, a + 1)
                    for u in range(2):
                        for t in range(NT):
                            m = pe.transpose(ps[:, 6, (u * NT + t) * P:(u * NT + t + 1) * P],
                                             y_sb[:, t, u * P:(u + 1) * P], ident[:, :])
                    m.then_inc(yT_made, 1)

            def project_pair(j, kind):
                for n in range(PAIR_HALVES):
                    if n == 0:
                        wait(pe, qk0_ready, j)
                        wait(pe, qk1_ready, j)
                    if n == PAIR_HALVES // 2:
                        if kind is None:
                            pe.wait_ge(gainsT_ready, 3)
                        wait(pe, v_ready, 2 * j)
                    within = n % (2 * NG)
                    if kind is None and n < 2 * NG:
                        pe.wait_ge(block_lo, n + 1)
                    half_group(PAIR_HALVES * j + n, n % SPLITS, (0, 1) if n < 2 * NG else (2, 3),
                               aT_hi, aT_lo, within * (GK // 2), within == 0, within == 2 * NG - 1)
                    if kind is None:
                        if n in (0, 2, 4):
                            transpose_block(1 + n // 2)
                        if n == 5:
                            pe.wait_ge(gains_loaded, 48)
                            pe.transpose(ps[:, 2, 0:2 * KO + 1], gains[:, :], ident[0:2 * KO + 1, 0:2 * KO + 1]
                                         ).then_inc(gainsT_made, 1)
                    else:
                        attend(n, j - 1, kind, 13)

            pe.wait_ge(ident_ready, 2)
            keep_busy(WARM_UP[0])
            pe.wait_ge(mix_gain_loaded, 16)
            pe.transpose(ps[:, 3, 0:KO], mix_gain[:, :], ident[0:KO, 0:KO]).then_inc(gainsT_made, 1)
            transpose_block(0)
            project_pair(0, None)
            with pe.Fori(1, KIND_PAIRS + 1) as j:
                project_pair(j, DIFF)
            with pe.Fori(KIND_PAIRS + 1, PAIRS) as j:
                project_pair(j, MOBA)

            banks_of = {("out", 0): (0, 1), ("out", 1): (2, 3), ("out", 2): (0, 1), ("out", 3): (2, 3),
                        ("qm", 0): (6, 7), ("km", 0): (0, 1), ("vm", 0): (2, 3)}
            operand = {"out": (yT_hi, yT_lo), "qm": (cT_hi, cT_lo), "km": (aT_hi, aT_lo),
                       "vm": (aT_hi, aT_lo)}
            for w, (what, n, g) in enumerate(TAIL):
                if (what, n, g) == ("out", 0, 0):
                    pe.wait_ge(qk0_ready, PAIRS)
                    pe.wait_ge(qk1_ready, PAIRS)
                if (what, n, g) == ("out", 1, 0):
                    pe.wait_ge(v_ready, 2 * PAIRS)
                if (what, n, g) == ("out", 2, 0):
                    pe.wait_ge(x1_ready, NT * 1)
                if (what, n, g) == ("out", 3, 0):
                    pe.wait_ge(x1_ready, NT * 2)
                if what == "km" and g == 0:
                    pe.wait_ge(x1_ready, NT * 3)
                if what == "vm" and g == 0:
                    pe.wait_ge(x1_ready, NT * 4)
                if what == "qm":
                    b = BLOCKS.index(("x1", g, 4))
                    pe.wait_ge(block_lo, 2 * (max(b, BLOCKS.index(("mem", 2, 6))) + 1))
                hi, lo = operand[what]
                for hf in range(2):
                    if (what, n, g, hf) == ("out", 0, 3, 1):
                        pe.wait_ge(yT_ready, PAIRS)
                    k0 = (g * GK if what in ("out", "km", "vm") else 0) + hf * (GK // 2)
                    half_group(TAIL_HALF0 + 2 * w + hf, (2 * w + hf) % SPLITS, banks_of[what, n], hi, lo, k0,
                               g == 0 and hf == 0, g == NG - 1 and hf == 1)
                    if 2 * w + hf <= 11:
                        attend(2 * w + hf, PAIRS - 1, MOBA, 11)
                if w in BLOCK_AFTER:
                    transpose_block(BLOCK_AFTER[w])
                if (what, n, g) == ("km", 0, 2):
                    pe.wait_ge(qm_ready, NT)
                    for h in range(4):
                        for t in range(NT):
                            m = pe.transpose(ps[:, 4 + h // 2, ((h % 2) * NT + t) * P:((h % 2) * NT + t + 1) * P],
                                             qm_sb[:, t, h * P:(h + 1) * P], ident[:, :])
                        if h % 2:
                            m.then_inc(qmT_made, 1)
                if (what, n, g) == ("vm", 0, 0):
                    pe.wait_ge(km_ready, NT)
                    for h in range(4):
                        for t in range(NT):
                            m = pe.transpose(ps[:, 6 + h // 2, ((h % 2) * NT + t) * P:((h % 2) * NT + t + 1) * P],
                                             km_sb[:, t, h * P:(h + 1) * P], ident[:, :])
                        if h % 2:
                            m.then_inc(kmT_made, 1)
                if (what, n, g) == ("vm", 0, 1):
                    pe.wait_ge(qmT_ready, 2)
                    pe.wait_ge(kmT_ready, 2)
                    for t in range(NT):
                        for h in range(4):
                            m = pe.matmul(ps[:, (4, 0)[t] + h // 2, (h % 2) * SEQ:(h % 2 + 1) * SEQ],
                                          qmT_sb[:, h, t * P:(t + 1) * P], kmT_sb[:, h, :], start=True, stop=True)
                        m.then_inc(scores_m_made, 1)
                if what == "vm" and g >= 2:
                    t = g - 2
                    pe.wait_ge(pm_ready, t + 1)
                    for kb in range(2):
                        for h in range(4):
                            m = pe.transpose(ps[:, (6, 4)[t] + kb, h * P:(h + 1) * P],
                                             pm_sb[:, t, h, kb * P:(kb + 1) * P], ident[:, :])
                        m.then_inc(pmT_made, 1)

            def memory_output(t):
                pe.wait_ge(pmT_ready[0], t + 1)
                pe.wait_ge(pmT_ready[1], t + 1)
                for h in range(4):
                    head = slice(h * P, (h + 1) * P)
                    for kb in range(2):
                        m = pe.matmul(ps[:, t, head], vm_sb[:, kb, head], pmT_sb[:, t, kb, h],
                                      start=kb == 0, stop=kb == 1)
                m.then_inc(omT_made, 1)

            def project_output(t, piece):
                col, width, bank = WO_PIECES[t][piece]
                tok = slice(t * P, (t + 1) * P)
                acc = ps[:, bank, 0:width]
                before = [b for _, _, b in WO_PIECES[0]]
                if t == 1 and bank in before:
                    pe.wait_ge(x2_ready, before.index(bank) + 1)
                if piece == 0:
                    pe.wait_ge(omT_hi_ready, t + 1)

                def split_rows(h):
                    half = 2 * (col // COLS) + h // 2
                    cols = slice(col % COLS, col % COLS + width)
                    if half < SPLITS:
                        return wo_hi[:, half, h % 2, cols], wo_lo[:, half, h % 2, cols]
                    return w_hi[:, half % SPLITS, h % 2, cols], w_lo[:, half % SPLITS, h % 2, cols]

                for h in range(4):
                    if t == 0 and h % 2 == 0:
                        pe.wait_ge(lo_made, TAIL_HALF0 + WO_HALF0 + 2 * piece + h // 2 + 1)
                    hi, lo = split_rows(h)
                    pe.matmul(acc, cT_hi[:, h, tok], hi, start=h == 0, stop=False)
                    pe.matmul(acc, cT_hi[:, h, tok], lo, start=False, stop=False)
                if piece == 0:
                    pe.wait_ge(omT_ready, t + 1)
                for h in range(4):
                    m = pe.matmul(acc, cT_lo[:, h, tok], split_rows(h)[0], start=False, stop=h == 3)
                m.then_inc(wo_done, 1)

            pe.wait_ge(vm_ready, NT)
            for t in range(NT):
                memory_output(t)
            for piece in range(len(WO_PIECES[0])):
                project_output(0, piece)
            for piece in range(len(WO_PIECES[1])):
                project_output(1, piece)

        @block.scalar
        def _(act):
            def split_hi(half, i, turn, tail=False):
                act.wait_ge(half_loaded[i % RAW], 32 * (turn + i // RAW + 1))
                raw = w_raw[:, i % RAW]
                if tail and i in range(WO_HALF0, WO_HALF0 + SPLITS):
                    act.activation(wo_hi[:, i - WO_HALF0], raw, ACT.Copy).then_inc(hi_made, 1)
                    return
                behind = 2 * SPLITS if tail and i >= WO_HALF0 else SPLITS
                wait(act, half_done, half - behind + 1)
                if isinstance(half, int) and half == 0:
                    act.activation(w_hi[:, 0, 0], raw[:, 0], ACT.Copy).then_inc(first_hi, 1)
                    act.activation(w_hi[:, 0, 1], raw[:, 1], ACT.Copy).then_inc(hi_made, 1)
                    return
                act.activation(w_hi[:, i % SPLITS], raw, ACT.Copy).then_inc(hi_made, 1)

            def block_hi_bank(b, i):
                source, n, bank = BLOCKS[b]
                first_gain = {"x": 0, "x1": KO, "mem": 2 * KO}[source]
                act.wait_ge(block_made, 2 * b + i + 1)
                for k in (2 * i, 2 * i + 1):
                    into = cT_hi[:, k] if source == "x1" else aT_hi[:, GK * n + k]
                    gain = first_gain + GK * n + k
                    m = act.activation(into, ps[:, bank + i, (k % 2) * SEQ:(k % 2 + 1) * SEQ], ACT.Identity,
                                       scale=gainsT[:, gain:gain + 1])
                m.then_inc(block_hi, 1)

            def chunk_b_out(a, t):
                gate = ps[:, 2 + t, 2 * P:4 * P]
                act.activation(sig_sb[:, t], gate, ACT.Exp, scale=neg_r_x[:, t:t + 1])
                act.activation(gate_sb[:, t], gate, ACT.Identity, scale=r_x[:, t:t + 1]).then_inc(gate_ready, 1)
                act.activation(v_parts[:, t, 0], ps[:, 2 + t, 0:2 * P], ACT.Identity, scale=r_x[:, t:t + 1]
                               ).then_inc(v_hi_ready, 1)

            def attend(n, a, kind):
                x_bank, y_bank = (6, 4), (7, 5)
                if n == 0:
                    act.wait_ge(half_done, PAIR_HALVES * (a + 1))
                    chunk_b_out(a, 0)
                if n == 1:
                    for i, (hi, scale) in enumerate(((qT_hi[:, :, :], kind.scale), (kT_parts[:, :, 0, :], 1.0))):
                        act.wait_ge(qkT_made, 2 * a + i + 1)
                        act.activation(hi, ps[:, 4 + i, :].rearrange("p (u s) -> p u s", s=SEQ), ACT.Copy,
                                       scale=scale).then_inc(qkT_hi_ready, 1)
                if n == 2:
                    chunk_b_out(a, 1)
                if n in (4, 5):
                    u = n - 4
                    act.wait_ge(max_ready, 2 * a + u + 1)
                    for c in range(kind.maps):
                        for t in (1, 0):
                            cols = slice(0, SEQ) if t == 1 else slice(SEQ, SEQ + P)
                            m = act.activation(prob_sb[:, u, c, cols], prob_sb[:, u, c, cols], ACT.Exp,
                                               bias=neg_max[:, u, t, c:c + 1],
                                               accum_out=exp_sum[:, c, u, t:t + 1])
                    m.then_inc(exp_ready, 1)
                if n in (7, 9):
                    u = (n - 7) // 2
                    act.wait_ge(probT_made, 2 * a + u + 1)
                    act.activation(probT_hi[:, u].rearrange("p i q -> p (i q)"), ps[:, x_bank[u], 0:3 * P],
                                   ACT.Copy).then_inc(probT_hi_ready, 1)
                if n in (10, 11) and kind.diff:
                    u = n - 10
                    act.wait_ge(o_ready, 2 * a + u + 1)
                    for t in range(NT):
                        m = act.activation(junk[:, (2 * u + t) * P:(2 * u + t + 1) * P],
                                           y_sb[:, t, u * P:(u + 1) * P],
                                           ACT.Square, accum_out=o_sq[:, u, t:t + 1])
                    m.then_inc(o_summed, 1)

            def qk1_out(j):
                act.wait_ge(half_done, PAIR_HALVES * j + PAIR_HALVES // 2)
                act.activation(qk_sb[:, 1], ps[:, 1, :], ACT.Identity, scale=r_x[:, 1:2]).then_inc(qk1_ready, 1)

            def pair_window(j, kind):
                for n in range(PAIR_HALVES):
                    split_hi(PAIR_HALVES * j + n + 2, n + 2, 2 * j)
                    attend(n, j - 1, kind)
                    if n == PAIR_HALVES // 2:
                        qk1_out(j)

            act.dma_start(mix_gain[:, :], norm_mix_g[0].rearrange("(k p) -> k p", p=P)).then_inc(mix_gain_loaded, 16)
            act.wait_ge(warm_ready, 1)
            act.activation(warm, warm, ACT.Exp).then_inc(warm_ready, 1)

            act.wait_ge(gainsT_ready, 1)
            block_hi_bank(0, 0)
            split_hi(0, 0, 0)
            block_hi_bank(0, 1)
            split_hi(1, 1, 0)
            block_hi_bank(1, 0)
            split_hi(2, 2, 0)
            block_hi_bank(1, 1)
            for n in range(PAIR_HALVES):
                if n in (3, 4, 5, 6):
                    block_hi_bank((n + 1) // 2, (n + 1) % 2)
                if n > 0:
                    split_hi(n + 2, n + 2, 0)
                if n == 6:
                    for part_loaded in x_loaded:
                        act.wait_ge(part_loaded, 16)
                if n in (6, 7):
                    act.activation(junk_row, xs[:, n - 6, :], ACT.Square,
                                   accum_out=x_sq[:, n - 6:n - 5]).then_inc(x_summed, 1)
                    act.wait_ge(x_summed, n - 5)
                if n == 12:
                    act.wait_ge(lam_dots, 2)
                    act.activation(lam_exp, lam_dot, ACT.Exp).then_inc(lam_exps, 1)
                if n == PAIR_HALVES // 2:
                    act.wait_ge(r_x_ready, 1)
                    qk1_out(0)
            with act.Fori(1, KIND_PAIRS + 1) as j:
                pair_window(j, DIFF)
            with act.Fori(KIND_PAIRS + 1, PAIRS) as j:
                pair_window(j, MOBA)

            block_half = {2 * w + 2: b for w, b in BLOCK_AFTER.items()}
            for i in range(2 * len(TAIL)):
                split_hi(TAIL_HALF0 + i + 2, i + 2, 2 * PAIRS, True)
                if i <= 11:
                    attend(i, PAIRS - 1, MOBA)
                if i in block_half:
                    block_hi_bank(block_half[i], 0)
                if i - 1 in block_half:
                    block_hi_bank(block_half[i - 1], 1)
                if i in (17, 19, 27, 39):
                    n = {17: 0, 19: 1, 27: 2, 39: 3}[i]
                    act.wait_ge(x1_ready, NT * (n + 1))
                    for t in range(NT):
                        m = act.activation(junk[:, :], xs[:, t, n * COLS:(n + 1) * COLS], ACT.Square,
                                           accum_out=x1_sq[:, t, n:n + 1])
                        m.then_inc(x1_summed, 1)
                        act.wait_ge(x1_summed, NT * n + t + 1)
                if i in range(28, 36):
                    t, q = (i - 28) // 4, i % 4
                    if i == 28:
                        act.wait_ge(mem_loaded, 16)
                    act.activation(junk[:, :], mems[:, t, q * COLS:(q + 1) * COLS], ACT.Square,
                                   accum_out=mem_sq4[:, t, q:q + 1]).then_inc(mem_summed, 1)
                    act.wait_ge(mem_summed, i - 27)
                if i == 44:
                    act.wait_ge(half_done, done_at("qm", 0, 3))
                    act.wait_ge(q_scale_ready, 1)
                    act.activation(qm_sb[:, 1], ps[:, 7, :], ACT.Identity, scale=q_scale[:, 1:2]
                                   ).then_inc(qm_ready, 1)
                if i == 46:
                    act.wait_ge(qmT_made, 1)
                    act.activation(qmT_sb[:, 0:2].rearrange("p h s -> p (h s)"), ps[:, 4, :], ACT.Copy
                                   ).then_inc(qmT_ready, 1)
                if i == 48:
                    act.wait_ge(half_done, done_at("km", 0, 3))
                    act.wait_ge(r_mem_steps, 2 + RSQRT_STEPS)
                    act.activation(km_sb[:, 1], ps[:, 1, :], ACT.Identity, scale=r_mem[:, 1:2]
                                   ).then_inc(km_ready, 1)
                if i == 50:
                    act.wait_ge(kmT_made, 1)
                    act.activation(kmT_sb[:, 0:2].rearrange("p h s -> p (h s)"), ps[:, 6, :], ACT.Copy
                                   ).then_inc(kmT_ready, 1)
                if i in (53, 54):
                    t = i - 53
                    act.wait_ge(max_m_ready, t + 1)
                    for h in range(4):
                        m = act.activation(pm_sb[:, t, h], ps[:, (4, 0)[t] + h // 2, (h % 2) * SEQ:(h % 2 + 1) * SEQ],
                                           ACT.Exp, bias=neg_max_m[:, t, h:h + 1], accum_out=sum_m[:, t, h:h + 1])
                    m.then_inc(exp_m_ready, 1)
            for i in range(WO_HALF0 + 2, WO_HALF0 + SPLITS):
                split_hi(TAIL_HALF0 + i, i, 2 * PAIRS, True)
            for t in range(NT):
                if t == 1:
                    split_hi(TAIL_HALF0 + WO_HALF0 + SPLITS, WO_HALF0 + SPLITS, 2 * PAIRS, True)
                    act.wait_ge(half_done, done_at("vm", 0, 3))
                    act.activation(vm_sb[:, 1], ps[:, 3, :], ACT.Identity, scale=r_mem[:, 1:2]).then_inc(vm_ready, 1)
                act.wait_ge(pmT_made, 2 * t + 1)
                act.activation(pmT_sb[:, t, 0].rearrange("p h q -> p (h q)"), ps[:, (6, 4)[t], :], ACT.Copy
                               ).then_inc(pmT_ready[0], 1)
            split_hi(TAIL_HALF0 + WO_HALF0 + SPLITS + 1, WO_HALF0 + SPLITS + 1, 2 * PAIRS, True)
            for t in range(NT):
                act.wait_ge(omT_made, t + 1)
                act.activation(cT_hi[:, :, t * P:(t + 1) * P],
                               ps[:, t, :].rearrange("p (h q) -> p h q", q=P), ACT.Copy
                               ).then_inc(omT_hi_ready, 1)
                i = WO_HALF0 + SPLITS + 2 + t
                split_hi(TAIL_HALF0 + i, i, 2 * PAIRS, True)
            pieces = 0
            for t in range(NT):
                for n, (col, width, _) in enumerate(WO_PIECES[t]):
                    pieces += 1
                    act.wait_ge(x2_ready, pieces)
                    act.activation(junk[:, 0:width], xs[:, t, col:col + width], ACT.Square,
                                   accum_out=x2_sq[:, t, n:n + 1]).then_inc(x2_summed, 1)
                    act.wait_ge(x2_summed, pieces)
            act.wait_ge(x2_gained, pieces)
            act.wait_ge(r_x2_ready, NT)
            for q in (2, 3):
                cols = slice(q * COLS, (q + 1) * COLS)
                act.activation(result[:, 1, cols], result[:, 1, cols], ACT.Identity,
                               scale=r_x2[:, 1:2]).then_inc(out_ready[1], 1)

        @block.vector
        def _(dve):
            def split_lo(half, i, tail=False):
                over_yT = tail and i in range(WO_HALF0, WO_HALF0 + SPLITS)
                hi = wo_hi[:, i - WO_HALF0] if over_yT else w_hi[:, i % SPLITS]
                lo = wo_lo[:, i - WO_HALF0] if over_yT else w_lo[:, i % SPLITS]
                if isinstance(half, int) and half == 0:
                    dve.wait_ge(first_hi, 1)
                    dve.tensor_tensor(lo[:, 0], w_raw[:, 0, 0], hi[:, 0].bitcast(F32), ALU.subtract
                                      ).then_inc(first_lo, 1)
                    dve.wait_ge(hi_made, 1)
                    dve.tensor_tensor(lo[:, 1], w_raw[:, 0, 1], hi[:, 1].bitcast(F32), ALU.subtract
                                      ).then_inc(lo_made, 1)
                    return
                dve.wait_ge(hi_made, half + 1)
                dve.tensor_tensor(lo, w_raw[:, i % RAW], hi.bitcast(F32), ALU.subtract).then_inc(lo_made, 1)

            def block_lo_bank(b, i):
                source, n, bank = BLOCKS[b]
                first_gain = {"x": 0, "x1": KO, "mem": 2 * KO}[source]
                dve.wait_ge(block_hi, 2 * b + i + 1)
                for k in (2 * i, 2 * i + 1):
                    hi, lo = (cT_hi[:, k], cT_lo[:, k]) if source == "x1" else \
                             (aT_hi[:, GK * n + k], aT_lo[:, GK * n + k])
                    gain = first_gain + GK * n + k
                    m = dve.scalar_tensor_tensor(lo, ps[:, bank + i, (k % 2) * SEQ:(k % 2 + 1) * SEQ],
                                                 gainsT[:, gain:gain + 1], hi.bitcast(F32),
                                                 ALU.mult, ALU.subtract)
                m.then_inc(block_lo, 1)

            def rsqrt(y, a, scratch, steps, done):
                dve.tensor_scalar(y.bitcast(I32), a.bitcast(I32), -0.5, RSQRT_SEED, ALU.mult, ALU.add
                                  ).then_inc(steps, 1)
                for i in range(3):
                    dve.wait_ge(steps, done + 3 * i + 1)
                    dve.scalar_tensor_tensor(scratch, a, -0.5, y, ALU.mult, ALU.mult).then_inc(steps, 1)
                    dve.wait_ge(steps, done + 3 * i + 2)
                    dve.tensor_tensor(scratch, scratch, y, ALU.mult).then_inc(steps, 1)
                    dve.wait_ge(steps, done + 3 * i + 3)
                    dve.scalar_tensor_tensor(y, scratch, 1.5, y, ALU.add, ALU.mult).then_inc(steps, 1)
                dve.wait_ge(steps, done + RSQRT_STEPS)

            def silu_piece(a, i):
                t, half = i // 2, slice((i % 2) * P, (i % 2 + 1) * P)
                dve.wait_ge(gate_ready, 2 * a + t + 1)
                s, gate = sig_sb[:, t, half], gate_sb[:, t, half]
                dve.tensor_scalar(s, s, 1.0, None, ALU.add).then_inc(silu_steps, 1)
                dve.wait_ge(silu_steps, 12 * a + 3 * i + 1)
                dve.reciprocal(s, s).then_inc(silu_steps, 1)
                dve.wait_ge(silu_steps, 12 * a + 3 * i + 2)
                dve.tensor_tensor(gate, gate, s, ALU.mult).then_inc(silu_steps, 1)

            def attend(n, a, kind, y_out_at):
                x_bank, y_bank = (6, 4), (7, 5)
                local = a - kind.first_pair
                if n == 1:
                    for i, (hi, lo, scale) in enumerate(((qT_hi[:, :, :], qT_lo[:, :, :], kind.scale),
                                                         (kT_parts[:, :, 0, :], kT_parts[:, :, 1, :], 1.0))):
                        dve.wait_ge(qkT_hi_ready, 2 * a + i + 1)
                        dve.scalar_tensor_tensor(lo, ps[:, 4 + i, :].rearrange("p (u s) -> p u s", s=SEQ), scale,
                                                 hi.bitcast(F32),
                                                 ALU.mult, ALU.subtract).then_inc(qkT_ready, 1)
                if n in (2, 3):
                    t = n - 2
                    dve.wait_ge(v_hi_ready, 2 * a + t + 1)
                    dve.scalar_tensor_tensor(v_parts[:, t, 1], ps[:, 2 + t, 0:2 * P], r_x[:, t:t + 1],
                                             v_parts[:, t, 0].bitcast(F32), ALU.mult, ALU.subtract).then_inc(v_ready, 1)
                if n in (2, 6, 8, 10):
                    silu_piece(a, {2: 0, 6: 1, 8: 2, 10: 3}[n])
                if n in (3, 4):
                    u = n - 3
                    dve.wait_ge(scores_made, 2 * a + u + 1)
                    slope = slopes[:, bass.ds(2 * a + u, 1)]
                    banks = ps[:, x_bank[u]:x_bank[u] + kind.maps, :]
                    for cols, d in ((slice(SEQ, SEQ + P), slice(P, SEQ)), (slice(0, SEQ), slice(0, SEQ))):
                        width = cols.stop - cols.start
                        bias = dist[:, d].unsqueeze(1).to_broadcast([P, kind.maps, width])
                        dve.scalar_tensor_tensor(prob_sb[:, u, 0:kind.maps, cols], bias, slope,
                                                 banks[:, :, cols], ALU.mult, ALU.add).then_inc(logits_ready, 1)
                    tile0 = prob_sb[:, u, 0:kind.maps, SEQ:SEQ + P]
                    dve.wait_ge(logits_ready, 6 * a + 3 * u + 1)
                    dve.tensor_tensor(tile0, tile0, banks[:, :, SEQ + P:2 * SEQ], ALU.add).then_inc(logits_ready, 1)
                    for i, (t, cols) in enumerate(((1, slice(0, SEQ)), (0, slice(SEQ, SEQ + P)))):
                        dve.wait_ge(logits_ready, 6 * a + 3 * u + i + 2)
                        m = dve.tensor_reduce(neg_max[:, u, t, 0:kind.maps], prob_sb[:, u, 0:kind.maps, cols],
                                              axis=AX.X, op=ALU.max, negate=True)
                    m.then_inc(max_ready, 1)
                if n in (5, 6) and kind.diff:
                    u = n - 5
                    dve.wait_ge(exp_ready, 2 * a + u + 1)
                    dve.reciprocal(inv_sum1[:, u], exp_sum[:, 1, u]).then_inc(mix_steps, 1)
                    dve.wait_ge(mix_steps, 4 * local + 2 * u + 1)
                    dve.scalar_tensor_tensor(mix[:, u], inv_sum1[:, u], neg_lam[:, 0:1], exp_sum[:, 0, u],
                                             ALU.mult, ALU.mult).then_inc(mix_steps, 1)
                    dve.wait_ge(mix_steps, 4 * local + 2 * u + 2)
                    for t, cols in ((1, slice(0, SEQ)), (0, slice(SEQ, SEQ + P))):
                        m = dve.scalar_tensor_tensor(prob_sb[:, u, 0, cols], prob_sb[:, u, 1, cols],
                                                     mix[:, u, t:t + 1], prob_sb[:, u, 0, cols],
                                                     ALU.mult, ALU.add)
                    m.then_inc(attn_ready, 1)
                if n in (7, 9):
                    u = (n - 7) // 2
                    flat = "p i q -> p (i q)"
                    dve.wait_ge(probT_hi_ready, 2 * a + u + 1)
                    dve.tensor_tensor(probT_lo[:, u].rearrange(flat), ps[:, x_bank[u], 0:3 * P],
                                      probT_hi[:, u].rearrange(flat).bitcast(F32), ALU.subtract
                                      ).then_inc(probT_ready, 1)
                if n in (9, 11):
                    u = (n - 9) // 2
                    dve.wait_ge(pv_made, 2 * a + u + 1)
                    halves = ps[:, y_bank[u], :].rearrange("p (t i d) -> p t d i", i=2, d=P)
                    dve.tensor_reduce(y_sb[:, :, u * P:(u + 1) * P], halves, axis=AX.X, op=ALU.add
                                      ).then_inc(o_ready, 1)
                if n == 11:
                    steps = y_steps[kind.name]
                    if kind.diff:
                        done = local * (5 + RSQRT_STEPS)
                        dve.wait_ge(o_summed, 2 * local + 2)
                        dve.reciprocal(inv_sum0, exp_sum[:, 0]).then_inc(steps, 1)
                        dve.wait_ge(steps, done + 1)
                        dve.tensor_tensor(inv_sq, inv_sum0, inv_sum0, ALU.mult).then_inc(steps, 1)
                        dve.wait_ge(steps, done + 2)
                        dve.scalar_tensor_tensor(o_ms, o_sq, 1.0 / P, inv_sq, ALU.mult, ALU.mult
                                                 ).then_inc(steps, 1)
                        dve.wait_ge(steps, done + 3)
                        dve.tensor_scalar(o_ms, o_ms, EPS, None, ALU.add).then_inc(steps, 1)
                        dve.wait_ge(steps, done + 4)
                        flat = "p u t -> p (u t)"
                        rsqrt(r_o.rearrange(flat), o_ms.rearrange(flat), newton, steps, done + 4)
                        dve.tensor_tensor(y_scale, r_o, inv_sum0, ALU.mult).then_inc(steps, 1)
                        dve.wait_ge(steps, done + 5 + RSQRT_STEPS)
                    else:
                        dve.wait_ge(o_ready, 2 * a + 2)
                        dve.reciprocal(y_scale, exp_sum[:, 0]).then_inc(steps, 1)
                        dve.wait_ge(steps, local + 1)
                    dve.wait_ge(silu_steps, 12 * a + 12)
                    for u in range(2):
                        for t in range(NT):
                            head = slice(u * P, (u + 1) * P)
                            m = dve.scalar_tensor_tensor(y_sb[:, t, head], y_sb[:, t, head],
                                                         y_scale[:, u, t:t + 1], gate_sb[:, t, head],
                                                         ALU.mult, ALU.mult)
                    m.then_inc(y_ready, 1)
                if n == y_out_at:
                    gain = sub_gain[:, 0:1] if kind.diff else 1.0
                    hi = yT_hi[:, bass.ds(2 * a, 2), :]
                    lo = yT_lo[:, bass.ds(2 * a, 2), :]
                    yT = ps[:, 6, :].rearrange("p (u s) -> p u s", s=SEQ)
                    dve.wait_ge(yT_made, a + 1)
                    dve.tensor_scalar(hi, yT, gain, None, ALU.mult).then_inc(yT_hi_ready, 1)
                    dve.wait_ge(yT_hi_ready, a + 1)
                    dve.scalar_tensor_tensor(lo, yT, gain, hi.bitcast(F32), ALU.mult, ALU.subtract
                                             ).then_inc(yT_ready, 1)

            def qk0_out(j):
                dve.wait_ge(half_done, PAIR_HALVES * j + PAIR_HALVES // 2)
                dve.tensor_scalar(qk_sb[:, 0], ps[:, 0, :], r_x[:, 0:1], None, ALU.mult).then_inc(qk0_ready, 1)

            def pair_window(j, kind):
                for n in range(PAIR_HALVES):
                    split_lo(PAIR_HALVES * j + n + 2, n + 2)
                    attend(n, j - 1, kind, 14)
                    if n == PAIR_HALVES // 2:
                        qk0_out(j)

            def row_rms(sums, ms, r, steps, extra):
                dve.tensor_scalar(ms, sums, 1.0 / DM, EPS, ALU.mult, ALU.add).then_inc(steps, 1)
                dve.wait_ge(steps, extra + 1)
                rsqrt(r, ms, newton[:, 0:NT], steps, extra + 1)

            dve.wait_ge(gainsT_made, 1)
            dve.tensor_copy(gainsT[:, 0:KO], ps[:, 3, 0:KO]).then_inc(gainsT_ready, 1)
            dve.wait_ge(gainsT_ready, 1)
            block_lo_bank(0, 0)
            split_lo(0, 0)
            block_lo_bank(0, 1)
            split_lo(1, 1)
            block_lo_bank(1, 0)
            split_lo(2, 2)
            block_lo_bank(1, 1)
            for n in range(PAIR_HALVES):
                if n in (3, 4, 5, 6):
                    block_lo_bank((n + 1) // 2, (n + 1) % 2)
                if n > 0:
                    split_lo(n + 2, n + 2)
                if n == 6:
                    dve.wait_ge(gainsT_made, 2)
                    dve.tensor_copy(gainsT[:, KO:3 * KO + 1], ps[:, 2, 0:2 * KO + 1]).then_inc(gainsT_ready, 1)
                    dve.wait_ge(gainsT_ready, 2)
                    dve.tensor_scalar(sub_gain, gainsT[:, 3 * KO:3 * KO + 1], 1.0 - LAM_INIT, None, ALU.mult
                                      ).then_inc(gainsT_ready, 1)
                if n == 7:
                    dve.wait_ge(x_summed, NT)
                    row_rms(x_sq, x_ms, r_x, r_x_steps, 0)
                    dve.tensor_scalar(neg_r_x, r_x, -1.0, None, ALU.mult).then_inc(r_x_ready, 1)
                if n == 10:
                    dve.wait_ge(lam_loaded, 64)
                    for i in range(2):
                        dve.tensor_tensor(lam_prod[:, i], lam_in[:, 2 * i], lam_in[:, 2 * i + 1], ALU.mult
                                          ).then_inc(lam_steps, 1)
                    for i in range(2):
                        dve.wait_ge(lam_steps, i + 1)
                        dve.tensor_reduce(lam_dot[:, i:i + 1], lam_prod[:, i], axis=AX.X, op=ALU.add
                                          ).then_inc(lam_dots, 1)
                if n == PAIR_HALVES // 2:
                    qk0_out(0)
                if n == 14:
                    dve.wait_ge(lam_exps, 1)
                    dve.tensor_tensor(neg_lam, lam_exp[:, 1:2], lam_exp[:, 0:1], ALU.subtract).then_inc(lam_ready, 1)
                    dve.wait_ge(lam_ready, 1)
                    dve.tensor_scalar(neg_lam, neg_lam, -LAM_INIT, None, ALU.add).then_inc(lam_ready, 1)
                    dve.wait_ge(lam_ready, 2)
                    dve.wait_ge(consts_ready, CONSTS)
            with dve.Fori(1, KIND_PAIRS + 1) as j:
                pair_window(j, DIFF)
            with dve.Fori(KIND_PAIRS + 1, PAIRS) as j:
                pair_window(j, MOBA)

            block_half = {2 * w + 2: b for w, b in BLOCK_AFTER.items()}
            for i in range(2 * len(TAIL)):
                split_lo(TAIL_HALF0 + i + 2, i + 2, True)
                if i <= 12:
                    attend(i, PAIRS - 1, MOBA, 12)
                if i in block_half:
                    block_lo_bank(block_half[i], 0)
                if i - 1 in block_half:
                    block_lo_bank(block_half[i - 1], 1)
                if i in (14, 16, 26, 38):
                    n = {14: 0, 16: 1, 26: 2, 38: 3}[i]
                    dve.wait_ge(half_done, done_at("out", n, 3))
                    for t in range(NT):
                        cols = slice(n * COLS, (n + 1) * COLS)
                        dve.tensor_tensor(xs[:, t, cols], xs[:, t, cols], ps[:, 2 * (n % 2) + t, :], ALU.add
                                          ).then_inc(x1_ready, 1)
                if i == 36:
                    dve.wait_ge(mem_summed, 8)
                    dve.tensor_reduce(mem_sq, mem_sq4, axis=AX.X, op=ALU.add).then_inc(r_mem_steps, 1)
                    dve.wait_ge(r_mem_steps, 1)
                    row_rms(mem_sq, mem_ms, r_mem, r_mem_steps, 1)
                if i == 42:
                    dve.wait_ge(x1_summed, 4 * NT)
                    dve.tensor_reduce(x1_tot, x1_sq, axis=AX.X, op=ALU.add).then_inc(r_x1_steps, 1)
                    dve.wait_ge(r_x1_steps, 1)
                    row_rms(x1_tot, x1_ms, r_x1, r_x1_steps, 1)
                    dve.tensor_scalar(q_scale, r_x1, HEAD_SCALE, None, ALU.mult).then_inc(q_scale_ready, 1)
                    dve.wait_ge(q_scale_ready, 1)
                if i == 44:
                    dve.wait_ge(half_done, done_at("qm", 0, 3))
                    dve.tensor_scalar(qm_sb[:, 0], ps[:, 6, :], q_scale[:, 0:1], None, ALU.mult).then_inc(qm_ready, 1)
                if i == 46:
                    dve.wait_ge(qmT_made, 2)
                    dve.tensor_copy(qmT_sb[:, 2:4].rearrange("p h s -> p (h s)"), ps[:, 5, :]).then_inc(qmT_ready, 1)
                if i == 48:
                    dve.wait_ge(half_done, done_at("km", 0, 3))
                    dve.tensor_scalar(km_sb[:, 0], ps[:, 0, :], r_mem[:, 0:1], None, ALU.mult).then_inc(km_ready, 1)
                if i == 50:
                    dve.wait_ge(kmT_made, 2)
                    dve.tensor_copy(kmT_sb[:, 2:4].rearrange("p h s -> p (h s)"), ps[:, 7, :]).then_inc(kmT_ready, 1)
                if i in (54, 55):
                    t = i - 54
                    dve.wait_ge(exp_m_ready, t + 1)
                    dve.reciprocal(inv_sum_m[:, t], sum_m[:, t]).then_inc(inv_m_ready, 1)
                    dve.wait_ge(inv_m_ready, t + 1)
                    dve.tensor_tensor(pm_sb[:, t], pm_sb[:, t], inv_sum_m[:, t].unsqueeze(2).to_broadcast([P, 4, SEQ]),
                                      ALU.mult).then_inc(pm_ready, 1)
                if i == 52:
                    for t in range(NT):
                        dve.wait_ge(scores_m_made, t + 1)
                        banks = ps[:, (4, 0)[t]:(4, 0)[t] + 2, :].rearrange("p b (h k) -> p (b h) k", k=SEQ)
                        dve.tensor_reduce(neg_max_m[:, t], banks, axis=AX.X, op=ALU.max, negate=True
                                          ).then_inc(max_m_ready, 1)
            for i in range(WO_HALF0 + 2, WO_HALF0 + SPLITS):
                split_lo(TAIL_HALF0 + i, i, True)
            for t in range(NT):
                if t == 1:
                    dve.wait_ge(half_done, done_at("vm", 0, 3))
                    dve.tensor_scalar(vm_sb[:, 0], ps[:, 2, :], r_mem[:, 0:1], None, ALU.mult).then_inc(vm_ready, 1)
                dve.wait_ge(pmT_made, 2 * t + 2)
                dve.tensor_copy(pmT_sb[:, t, 1].rearrange("p h q -> p (h q)"), ps[:, (6, 4)[t] + 1, :]
                                ).then_inc(pmT_ready[1], 1)
            split_lo(TAIL_HALF0 + WO_HALF0 + SPLITS, WO_HALF0 + SPLITS, True)
            for t in range(NT):
                dve.wait_ge(omT_hi_ready, t + 1)
                tok = slice(t * P, (t + 1) * P)
                dve.tensor_tensor(cT_lo[:, :, tok], ps[:, t, :].rearrange("p (h q) -> p h q", q=P),
                                  cT_hi[:, :, tok].bitcast(F32), ALU.subtract).then_inc(omT_ready, 1)
                if t == 0:
                    i = WO_HALF0 + SPLITS + 1
                    split_lo(TAIL_HALF0 + i, i, True)
            for i in range(WO_HALF0 + SPLITS + 2, WO_HALF0 + 2 * SPLITS):
                split_lo(TAIL_HALF0 + i, i, True)
            dve.wait_ge(final_g_loaded, 16)
            pieces = 0
            for t in range(NT):
                column = slice(t, t + 1)
                last = len(WO_PIECES[t]) - 1
                for n, (col, width, bank) in enumerate(WO_PIECES[t]):
                    pieces += 1
                    dve.wait_ge(wo_done, pieces)
                    cols = slice(col, col + width)
                    dve.tensor_tensor(xs[:, t, cols], xs[:, t, cols], ps[:, bank, 0:width], ALU.add
                                      ).then_inc(x2_ready, 1)
                    dve.wait_ge(x2_ready, pieces)
                    dve.tensor_tensor(result[:, t, cols], xs[:, t, cols], final_gs[:, cols], ALU.mult
                                      ).then_inc(x2_gained, 1)
                    if n == last - 1:
                        dve.wait_ge(x2_summed, pieces)
                        dve.tensor_reduce(x2_tot[:, column], x2_sq[:, t, 0:last], axis=AX.X, op=ALU.add
                                          ).then_inc(r_x2_steps, 1)
                        dve.wait_ge(r_x2_steps, 9 * t + 1)
                        dve.tensor_scalar(x2_base[:, column], x2_tot[:, column], 1.0 / DM, EPS, ALU.mult, ALU.add
                                          ).then_inc(r_x2_steps, 1)
                a, half, y, s = x2_ms[:, column], x2_half[:, column], r_x2[:, column], newton[:, column]
                dve.wait_ge(r_x2_steps, 9 * t + 2)
                dve.wait_ge(x2_summed, pieces)
                dve.tensor_scalar(a, x2_sq[:, t, last:last + 1], 1.0 / DM, x2_base[:, column], ALU.mult, ALU.add
                                  ).then_inc(r_x2_steps, 1)
                dve.wait_ge(r_x2_steps, 9 * t + 3)
                dve.tensor_scalar(half, a, -0.5, None, ALU.mult)
                dve.tensor_scalar(y.bitcast(I32), a.bitcast(I32), -0.5, RSQRT_SEED, ALU.mult, ALU.add
                                  ).then_inc(r_x2_steps, 1)
                for i in range(3):
                    dve.wait_ge(r_x2_steps, 9 * t + 4 + 2 * i)
                    dve.scalar_tensor_tensor(s, half, y, y, ALU.mult, ALU.mult).then_inc(r_x2_steps, 1)
                    dve.wait_ge(r_x2_steps, 9 * t + 5 + 2 * i)
                    dve.scalar_tensor_tensor(y, s, 1.5, y, ALU.add, ALU.mult
                                             ).then_inc(r_x2_steps if i < 2 else r_x2_ready, 1)
                dve.wait_ge(r_x2_ready, t + 1)
                dve.wait_ge(x2_gained, pieces)
                for cols in (slice(0, DM),) if t == 0 else (slice(0, COLS), slice(COLS, 2 * COLS)):
                    dve.tensor_scalar(result[:, t, cols], result[:, t, cols], y, None, ALU.mult
                                      ).then_inc(out_ready[0], 1)


_INS = ["x", "mem", "norm_mix_g", "w_in", "lambda_q1", "lambda_k1", "lambda_q2", "lambda_k2",
        "subln_g", "w_out", "norm_mem_g", "mem_norm_g", "w_q_mem", "w_kv_mem", "w_o_mem", "final_g"]


def kernel(**inputs):
    import numpy as np
    import concourse.bacc as bacc
    from concourse.bass_utils import run_bass_kernel_spmd as run

    nc = bacc.Bacc("TRN2", target_bir_lowering=False, num_devices=1)
    arrays, args = {}, []
    for name in _INS:
        a = np.ascontiguousarray(inputs[name])
        arrays[f"in_{name}"] = a
        args.append(nc.dram_tensor(f"in_{name}", a.shape, mybir.dt.from_np(a.dtype), kind="ExternalInput").ap())
    out = nc.dram_tensor("out", (1, SEQ, DM), F32, kind="ExternalOutput").ap()
    program(nc, *args, out)
    r = run(nc, [arrays], core_ids=[0])
    return r.results[0]["out"]
```
